# Optimizing a Trainium2 kernel written in Bass

```python
import jax
import jax.numpy as jnp
from jax import lax

D_MODEL = 1024
BATCH = 1
SEQ = 512
DEPTH = 2
DEC_BATCH = 8
DEC_SEQ = 8
PAST_LEN = 2048
PAGE_SIZE = 128

N_HEADS = D_MODEL // 64
QK_NOPE = 64
QK_ROPE = 32
V_HEAD = 64
KV_LORA = D_MODEL // 4
Q_LORA = 3 * D_MODEL // 4
LATENT = KV_LORA + QK_ROPE
ROPE_THETA = 10000.0
ATTN_SCALE = (QK_NOPE + QK_ROPE) ** -0.5
Q_BLOCK = 128
D_POOL = D_MODEL
POOL_WINDOWS = (2, 4, 8, 16)
N_POOL_GROUPS = 4
POOL_GW = D_POOL // N_POOL_GROUPS
POOL_CTX = 15
D_FF = ((8 * D_MODEL // 3 + 127) // 128) * 128
CONV_W = 3
N_IN = Q_LORA + KV_LORA + QK_ROPE + D_POOL + 2 * D_MODEL
EPS = 1e-6

kernel_name = 'hybrid_pool_mla_convffn_decoder_step'

def _rmsnorm(x, g):
    x32 = x.astype(jnp.float32)
    y = x32 * lax.rsqrt(jnp.mean(x32 * x32, axis=-1, keepdims=True) + EPS) * g.astype(jnp.float32)
    return y.astype(x.dtype)

def _rope(x, pos):
    half = x.shape[-1] // 2
    freq = ROPE_THETA ** (-jnp.arange(half, dtype=jnp.float32) / half)
    ang = pos[:, None] * freq[None, :]
    shape = (1, x.shape[1]) + (1,) * (x.ndim - 3) + (half,)
    cos = jnp.cos(ang).reshape(shape)
    sin = jnp.sin(ang).reshape(shape)
    x32 = x.astype(jnp.float32)
    x1, x2 = x32[..., :half], x32[..., half:]
    return jnp.concatenate([x1 * cos - x2 * sin, x1 * sin + x2 * cos], axis=-1).astype(x.dtype)

def _causal_attention(q, k, v, q_pos, k_pos, s_spec, o_spec):
    B, Sq = q.shape[:2]
    blk = Q_BLOCK if Sq % Q_BLOCK == 0 else Sq
    nb = Sq // blk
    qb = jnp.moveaxis(q.reshape((B, nb, blk) + q.shape[2:]), 1, 0)
    pb = q_pos.reshape(nb, blk)

    def one_block(args):
        qi, pi = args
        s = jnp.einsum(s_spec, qi, k).astype(jnp.float32) * ATTN_SCALE
        s = jnp.where(k_pos[None, None, None, :] <= pi[None, None, :, None], s, -1e30)
        p = jax.nn.softmax(s, axis=-1).astype(v.dtype)
        return jnp.einsum(o_spec, p, v)

    o = jnp.moveaxis(lax.map(one_block, (qb, pb)), 0, 1)
    return o.reshape((B, Sq) + o.shape[3:])

def _pool_mixer(u, prev, pos, w_pool, pool_scale):
    B, S, _ = u.shape
    P = prev.shape[1]
    ext = jnp.concatenate([prev, u], axis=1)
    cs = jnp.cumsum(ext.astype(jnp.float32), axis=1)
    cs = jnp.concatenate([jnp.zeros((B, 1, D_POOL), jnp.float32), cs], axis=1)
    ys = []
    for g, w in enumerate(POOL_WINDOWS):
        sl = slice(g * POOL_GW, (g + 1) * POOL_GW)
        hi = cs[:, P + 1:P + S + 1, sl]
        lo = cs[:, P + 1 - w:P + S + 1 - w, sl]
        cnt = jnp.minimum(pos + 1.0, float(w))
        ys.append((hi - lo) / cnt[None, :, None] - u[..., sl].astype(jnp.float32))
    y = jnp.stack(ys, axis=2).astype(u.dtype)
    z = jnp.einsum('bsgi,gio->bsgo', y, w_pool).reshape(B, S, D_POOL)
    return z * pool_scale, ext[:, -POOL_CTX:]

def _causal_dwconv(z, prev, w_conv, b_conv):
    S = z.shape[1]
    ext = jnp.concatenate([prev, z], axis=1)
    out = b_conv + sum(ext[:, t:t + S] * w_conv[t] for t in range(CONV_W))
    return out, ext[:, -(CONV_W - 1):]

def _layer(x, c, pos0, past, pool_prev, conv_prev, lw):
    B, S, _ = x.shape
    pos_i = pos0 + jnp.arange(S, dtype=jnp.int32)
    pos_f = pos_i.astype(jnp.float32)
    mod = c @ lw['w_ada'] + lw['b_ada']
    sh1, sc1, g1, sh2, sc2, g2 = [m[:, None, :] for m in jnp.split(mod, 6, axis=-1)]

    h = _rmsnorm(x, lw['g_attn']) * (1 + sc1) + sh1
    proj = h @ lw['w_in']
    o1 = Q_LORA
    o2 = o1 + KV_LORA
    o3 = o2 + QK_ROPE
    o4 = o3 + D_POOL
    cq, ckv, kr, u, gates = proj[..., :o1], proj[..., o1:o2], proj[..., o2:o3], proj[..., o3:o4], proj[..., o4:]

    q = (_rmsnorm(cq, lw['g_q']) @ lw['w_uq']).reshape(B, S, N_HEADS, QK_NOPE + QK_ROPE)
    q_nope = q[..., :QK_NOPE]
    q_rope = _rope(q[..., QK_NOPE:], pos_f)
    latent = jnp.concatenate([_rmsnorm(ckv, lw['g_kv']), _rope(kr, pos_f)], axis=-1)
    if past is None:
        c_lat = latent[..., :KV_LORA]
        k_nope = jnp.einsum('bkc,chn->bkhn', c_lat, lw['w_uk'])
        k_rope = jnp.broadcast_to(latent[:, :, None, KV_LORA:], (B, S, N_HEADS, QK_ROPE))
        k = jnp.concatenate([k_nope, k_rope], axis=-1)
        v = jnp.einsum('bkc,chv->bkhv', c_lat, lw['w_uv'])
        o = _causal_attention(jnp.concatenate([q_nope, q_rope], axis=-1), k, v, pos_i, pos_i,
                              'bqhd,bkhd->bhqk', 'bhqk,bkhd->bqhd')
    else:
        keys = jnp.concatenate([past, latent], axis=1)
        k_pos = jnp.arange(keys.shape[1], dtype=jnp.int32)
        q_lat = jnp.einsum('bqhn,chn->bqhc', q_nope, lw['w_uk'])
        o_lat = _causal_attention(jnp.concatenate([q_lat, q_rope], axis=-1), keys, keys[..., :KV_LORA],
                                  pos_i, k_pos, 'bqhd,bkd->bhqk', 'bhqk,bkd->bqhd')
        o = jnp.einsum('bqhc,chv->bqhv', o_lat, lw['w_uv'])
    b_out = o.reshape(B, S, N_HEADS * V_HEAD)

    a_out, pool_new = _pool_mixer(u, pool_prev, pos_f, lw['w_pool'], lw['pool_scale'])

    gate = jax.nn.sigmoid(gates)
    mixed = (gate[..., :D_MODEL] * a_out + gate[..., D_MODEL:] * b_out) @ lw['w_out']
    x = x + g1 * mixed

    h2 = _rmsnorm(x, lw['g_ffn']) * (1 + sc2) + sh2
    z, conv_new = _causal_dwconv(h2 @ lw['w_up'], conv_prev, lw['w_conv'], lw['b_conv'])
    zg, zv = z[..., :D_FF], z[..., D_FF:]
    x = x + g2 * ((jax.nn.silu(zg) * zv) @ lw['w_down'])
    return x, latent, pool_new, conv_new

def setup_inputs(seed: int = 0) -> dict:
    key = jax.random.key(seed)
    ks = iter(list(jax.random.split(key, 32)))

    def nrm(shape, scale=1.0):
        return jax.random.normal(next(ks), shape, jnp.float32) * scale

    def gain(shape):
        return 1.0 + nrm(shape, 0.01)

    n_pages = PAST_LEN // PAGE_SIZE
    n_used = DEC_BATCH * n_pages
    n_phys = n_used + n_used // 4
    return {
        'x_prompt': nrm((BATCH, SEQ, D_MODEL)),
        'x_sample': nrm((DEC_BATCH, DEC_SEQ, D_MODEL)),
        'cache_latent': nrm((DEPTH, n_phys, PAGE_SIZE, LATENT)),
        'state_pool': nrm((DEPTH, DEC_BATCH, POOL_CTX, D_POOL)),
        'state_conv': nrm((DEPTH, DEC_BATCH, CONV_W - 1, 2 * D_FF)),
        'page_table': jax.random.permutation(next(ks), n_phys)[:n_used].reshape(DEC_BATCH, n_pages).astype(jnp.int32),
        'c_prompt': nrm((BATCH, D_MODEL)),
        'c_sample': nrm((DEC_BATCH, D_MODEL)),
        'w_ada': nrm((DEPTH, D_MODEL, 6 * D_MODEL), 0.5 * D_MODEL ** -0.5),
        'b_ada': nrm((DEPTH, 6 * D_MODEL), 0.01),
        'g_attn': gain((DEPTH, D_MODEL)),
        'w_in': nrm((DEPTH, D_MODEL, N_IN), D_MODEL ** -0.5),
        'g_q': gain((DEPTH, Q_LORA)),
        'w_uq': nrm((DEPTH, Q_LORA, N_HEADS * (QK_NOPE + QK_ROPE)), Q_LORA ** -0.5),
        'g_kv': gain((DEPTH, KV_LORA)),
        'w_uk': nrm((DEPTH, KV_LORA, N_HEADS, QK_NOPE), KV_LORA ** -0.5),
        'w_uv': nrm((DEPTH, KV_LORA, N_HEADS, V_HEAD), KV_LORA ** -0.5),
        'w_pool': nrm((DEPTH, N_POOL_GROUPS, POOL_GW, POOL_GW), POOL_GW ** -0.5),
        'pool_scale': gain((DEPTH, D_POOL)),
        'w_out': nrm((DEPTH, D_MODEL, D_MODEL), D_MODEL ** -0.5),
        'g_ffn': gain((DEPTH, D_MODEL)),
        'w_up': nrm((DEPTH, D_MODEL, 2 * D_FF), D_MODEL ** -0.5),
        'w_conv': nrm((DEPTH, CONV_W, 2 * D_FF), CONV_W ** -0.5),
        'b_conv': nrm((DEPTH, 2 * D_FF), 0.01),
        'w_down': nrm((DEPTH, D_FF, D_MODEL), D_FF ** -0.5),
        'g_final': gain((D_MODEL,)),
    }

def reference(x_prompt, x_sample, cache_latent, state_pool, state_conv, page_table, c_prompt, c_sample,
              w_ada, b_ada, g_attn, w_in, g_q, w_uq, g_kv, w_uk, w_uv, w_pool, pool_scale, w_out,
              g_ffn, w_up, w_conv, b_conv, w_down, g_final):
    n_pages = PAST_LEN // PAGE_SIZE
    n_seq = x_sample.shape[0]
    yp, ys = x_prompt, x_sample
    lat_p, pool_p, conv_p, lat_s, pool_s, conv_s = [], [], [], [], [], []
    for l in range(DEPTH):
        lw = dict(w_ada=w_ada[l], b_ada=b_ada[l], g_attn=g_attn[l], w_in=w_in[l], g_q=g_q[l], w_uq=w_uq[l],
                  g_kv=g_kv[l], w_uk=w_uk[l], w_uv=w_uv[l], w_pool=w_pool[l], pool_scale=pool_scale[l],
                  w_out=w_out[l], g_ffn=g_ffn[l], w_up=w_up[l], w_conv=w_conv[l], b_conv=b_conv[l],
                  w_down=w_down[l])
        pool0 = jnp.zeros((yp.shape[0], POOL_CTX, D_POOL), yp.dtype)
        conv0 = jnp.zeros((yp.shape[0], CONV_W - 1, 2 * D_FF), yp.dtype)
        yp, lp, pp, cp = _layer(yp, c_prompt, 0, None, pool0, conv0, lw)
        past = cache_latent[l][page_table].reshape(n_seq, n_pages * PAGE_SIZE, LATENT)
        ys, ls, ps, cs = _layer(ys, c_sample, PAST_LEN, past, state_pool[l], state_conv[l], lw)
        lat_p.append(lp)
        pool_p.append(pp)
        conv_p.append(cp)
        lat_s.append(ls)
        pool_s.append(ps)
        conv_s.append(cs)
    y_prompt = _rmsnorm(yp, g_final)
    y_sample = _rmsnorm(ys, g_final)
    return (y_prompt, y_sample, jnp.stack(lat_p), jnp.stack(pool_p), jnp.stack(conv_p),
            jnp.stack(lat_s), jnp.stack(pool_s), jnp.stack(conv_s))


_drawn_inputs = setup_inputs


def setup_inputs(seed=0):
    import zlib

    import numpy as np

    out = dict(_drawn_inputs(seed))
    spreads = {}
    factors = {'cache_latent': 4.098,
     'b_ada': 3.213,
     'g_attn': 5.98,
     'g_q': 27.622,
     'g_kv': 27.04,
     'pool_scale': 24.2,
     'g_ffn': 19.848,
     'b_conv': 22.733,
     'g_final': 30.28}
    for name, (base, spread) in spreads.items():
        noise = np.random.default_rng([zlib.crc32(name.encode()), seed]).standard_normal(out[name].shape)
        drawn = base * np.exp(spread * noise) if base else spread * noise
        out[name] = jnp.asarray(drawn.astype(out[name].dtype))
    for name, factor in factors.items():
        out[name] = (out[name] * factor).astype(out[name].dtype)
    return out
```

```python
import numpy as np
import concourse.bass as bass
from concourse import mybir

F32 = mybir.dt.float32
F32R = mybir.dt.float32r
I32 = mybir.dt.int32
ALU = mybir.AluOpType
ACT = mybir.ActivationFunctionType
AX = mybir.AxisListType

D = 1024
DEPTH = 2
TP, NB, NS = 512, 8, 8
TS = NB * NS
T = TP + TS
HT = T // 2
PAST, PAGE = 2048, 128
NPG = PAST // PAGE
NH, DN, DR, DV = 16, 64, 32, 64
KVL, QL = 256, 768
LAT = KVL + DR
SCALE = float((DN + DR) ** -0.5)
WINDOWS = (2, 4, 8, 16)
CTX = 15
DF = 2816
EPS = 1e-6
KD, KQ, KF = D // 128, QL // 128, DF // 128
KC = KVL // 128
UE = CTX + TP + NB * (CTX + NS)
US = CTX + TP
ZE = 2 + TP + NB * (2 + NS)
ZS = 2 + TP
NC = 1 + NB

U_ADA, U_CQ, U_KV, U_KR, U_U = 0, 48, 54, 56, 58
U_QN, U_QR, U_POOL, U_G, U_UK, U_UV, U_OUT, U_UP, U_DOWN, UNITS = 66, 74, 78, 80, 96, 98, 100, 108, 152, 176

C_KV, C_KR, C_U, C_G = QL, QL + KVL, QL + KVL + DR, QL + KVL + DR + D

P_GA, P_GF, P_PS, P_BA, P_GQ, P_GK, P_ALL = 0, 8, 16, 24, 72, 78, 80


class Signal:

    def __init__(self, sem, per_layer, ahead=0):
        self.sem, self.per_layer, self.ahead = sem, per_layer, ahead

    def at(self, l, k):
        return l * self.per_layer + (k + self.ahead)


def build(nc, A, O):
    base = 16512
    place = [base]

    def keep(name, shape, dt=F32):
        size = int(np.prod(shape[1:])) * 4
        t = nc.alloc_sbuf_tensor_at(name, shape, dt, offset=place[0])
        place[0] += (size + 31) // 32 * 32
        return t

    x = keep("x", [128, KD, T])
    raw = keep("raw", [128, 2, 1024])
    whi = keep("whi", [128, 2, 1024], F32R)
    wlo = keep("wlo", [128, 2, 1024], F32R)
    ident = keep("ident", [128, 128])
    ident_r = keep("ident_r", [128, 128], F32R)
    ones = keep("ones", [128, 128])
    causal = keep("causal", [128, 128])
    causal_s = keep("causal_s", [128, NS])
    fold = keep("fold", [2 * NC, NC])
    ramp = keep("ramp", [128, 4, 16])
    par = keep("par", [128, P_ALL])
    convp = keep("convp", [128, 2, 2 * 2 * KF])
    conv_prev = keep("conv_prev", [128, 2 * NB, 2 * KF])
    mod = keep("mod", [128, 6 * KD, NC])
    gain1 = keep("gain1", [128, KD, NC])
    gain2 = keep("gain2", [128, KD, NC])
    cond = keep("cond", [128, KD, 2 * NC], F32R)
    g_fin = keep("g_fin", [128, KD])
    eps = keep("eps", [128, 1])
    softm = keep("softm", [128, 32])
    tab = keep("tab", [1, NB * NPG], I32)
    ada_rows = keep("ada_rows", [2 * NC, 2, 128])
    work = place[0]
    sumsq = keep("sumsq", [128, T])
    rinv = keep("rinv", [128, T])
    tmp = keep("tmp", [128, 2, T])
    arena = place[0]

    def at(name, shape, off, dt=F32):
        return nc.alloc_sbuf_tensor_at(name, shape, dt, offset=off)

    B = T * 4
    h_hi = at("h_hi", [128, KD, T], arena, F32R)
    h_lo = at("h_lo", [128, KD, T], arena + KD * B, F32R)
    a = arena + 2 * KD * B
    uext = at("uext", [128, KD, UE], a)
    a += KD * UE * 4
    cq_at = a
    cq_hi = at("cq_hi", [128, KQ, T], a, F32R)
    cq = at("cq", [128, KQ, T], a + KQ * B)
    cq_lo = at("cq_lo", [128, KQ, T], a + KQ * B, F32R)
    a += 2 * KQ * B
    y0_at = a
    a += 4 * B
    ckv_at = a
    ckv_hi = at("ckv_hi", [128, KC, T], a, F32R)
    ckv_lo = at("ckv_lo", [128, KC, T], a + KC * B, F32R)
    a += 2 * KC * B
    ckv = at("ckv", [128, KC, T], a)
    a += KC * B
    krope = at("krope", [DR, T], a)
    a += B
    q_at = a
    qn = at("qn", [128, KD, T], a)
    qr = at("qr", [128, 4, T], a + KD * B)
    a += 12 * B
    end_at = a
    rope = at("rope", [128, 2, T], a)
    a += 2 * B
    assert a <= 229344, a
    y_hi = [at(f"y_hi{g}", [128, 2, T], o, F32R) for g, o in enumerate((y0_at, cq_at, cq_at + 4 * B, cq_at + 8 * B))]
    y_lo = [at(f"y_lo{g}", [128, 2, T], o + 2 * B, F32R)
            for g, o in enumerate((y0_at, cq_at, cq_at + 4 * B, cq_at + 8 * B))]
    win = at("win", [128, 2, UE], work)
    win2 = [None] + [at(f"win2_{g}", [128, 2, UE], o) for g, o in enumerate((cq_at, cq_at + 4 * B, cq_at + 8 * B), 1)]
    kv_sum = at("kv_sum", [128, 2, T], q_at + 9 * B)
    rows = at("rows", [128, 17, 128], q_at)
    pool_prev = at("pool_prev", [128, NB * CTX, KD], q_at + 17 * 512)
    pool_last = at("pool_last", [128, KD, CTX + NB * CTX], q_at)
    pool_rows = at("pool_rows", [128, 2, 2, 512], q_at + 8 * 135 * 4 + 64)
    lat_rows = at("lat_rows", [128, 5, LAT], q_at + 12608)
    gate_b = at("gate_b", [128, KD, T], cq_at)
    kn = at("kn", [128, KD, TP], arena)
    wukT = at("wukT", [128, KD, KVL], arena + 16384)
    qlat = at("qlat", [128, KC, NB, NH, NS], arena + 24576)
    qrs = at("qrs", [DR, NB, NH, NS], arena + 32768)
    vn = at("vn", [128, 4, NH * DV], cq_at + KD * B)
    q96 = at("q96", [96, 2, TP], ckv_at)
    k96 = at("k96", [96, 2, TP], ckv_at + 4096)
    NP = 1280
    prob = at("prob", [128, NP], work)
    v64 = at("v64", [128, 2, 4, DV], work + NP * 4)
    probT = at("probT", [128, NP], end_at)
    pages = [at("pages0", [128, NPG, LAT], arena), at("pages1", [128, NPG, LAT], cq_at + KD * B)]
    keysT = [at("keysT0", [128, 3, 512], arena + 18432), at("keysT1", [128, 3, 512], ckv_at)]
    KS = PAST + NS
    sc = at("sc", [128, KS], end_at)
    pT = at("pT", [128, NPG + 1, 128], work)
    wuv = at("wuv", [128, KC, NH * DV], q_at)
    olatT = at("olatT", [128, KC, NH, NB, NS], q_at + 8192)
    olat = at("olat", [128, KVL], q_at + 16384)
    newk = at("newk", [NS, 2, LAT], q_at + 16384 + 1024)
    qst = at("qst", [128, 2, 3, 128], q_at + 16384 + 1024 + 2304)
    assert 16384 + 1024 + 2304 + 3072 <= 12 * B
    a = arena + 2 * KD * B
    act_hi = at("act_hi", [128, KF, T], a, F32R)
    act_lo = at("act_lo", [128, KF, T], a + KF * B, F32R)
    a += 2 * KF * B
    conv = at("conv", [128, 2, ZE], a)
    a += (2 * ZE * 4 + 31) // 32 * 32
    conv_last = at("conv_last", [128, 2 * KF, 2 * NC], a)
    a += 2 * KF * 2 * NC * 4
    assert a <= 229344, a
    zext = at("zext", [128, 2, ZE], work)
    conv_rows = at("conv_rows", [2 * NC, 2, 512], work + (2 * ZE * 4 + 31) // 32 * 32)
    rows_in = at("rows_in", [128, 5, D], arena)
    c_rows = at("c_rows", [NC, D], arena + 20480)
    cT = at("cT", [128, KD, NC], arena + 24576)
    gf_rows = at("gf_rows", [KD, 128], arena + 28672)
    yT = at("yT", [128, KD, T], arena)
    y_rows = at("y_rows", [128, 2, D], arena + KD * B)

    PS = nc.alloc_psum_tensor("PS", [128, 8, 512], F32)

    def signal(name, per_layer=0, ahead=0):
        return Signal(nc.alloc_semaphore(name), per_layer, ahead)

    def loads_before(u):
        return sum(2 if U_QN <= w < U_QR else 4 if U_QR <= w < U_POOL else 1 for w in range(u % 2, u, 2))

    LOADS = loads_before(UNITS)
    assert LOADS == loads_before(UNITS + 1)
    loaded = [signal("loaded0"), signal("loaded1")]
    hi_ready = signal("hi_ready", UNITS)
    lo_ready = signal("lo_ready", UNITS, 2)
    unit_used = signal("unit_used", UNITS, 2)

    N_TILE = dict(qkv=10, u=8, uq=12, pool=8, g=16, uk=8, uv=4, out=8, up=44, down=8)
    full = {k: signal(f"full_{k}", N_TILE[k]) for k in ("pool", "uk", "uv")}
    free = {k: signal(f"free_{k}", n, 2) for k, n in N_TILE.items()}
    const_in, x_in, tab_in = signal("const_in"), signal("x_in"), signal("tab_in")
    eps_set, start_T, start_ev = signal("eps_set"), signal("start_T"), signal("start_ev")
    cond_hi, cond_ready = signal("cond_hi"), signal("cond_ready")
    fin_norm, fin_T, fin_ev = signal("fin_norm"), signal("fin_T"), signal("fin_ev")
    y_out = [signal("y_out0"), signal("y_out1")]
    PAR_LOADS = 13
    par_in, rope_in = signal("par_in", 16 * PAR_LOADS), signal("rope_in", 16)
    par_T, par_ev = signal("par_T", 1), signal("par_ev", 1)
    ada_ev, ada_T, mod_ready = signal("ada_ev", 48), signal("ada_T", 48, 2), signal("mod_ready", 1)
    sq, sq_used = signal("sq", 2 * KD), signal("sq_used", 2 * KD, 2)
    ssum, ssum_p, root = signal("ssum", 4), signal("ssum_p", 4), signal("root", 4)
    scaled, affine, h_ready = signal("scaled", 2 * KD), signal("affine", 2 * KD), signal("h_ready", 2)
    cqn, ckvn = signal("cqn", 1), signal("ckvn", 1)
    lat_T, lat_ev, lat_out = signal("lat_T", 5), signal("lat_ev", 5), signal("lat_out", 32)
    last_ready, last_T, last_ev, last_out = signal("last_ready", 1), signal("last_T", 1), signal("last_ev", 1), signal("last_out", 32)
    y_ready, q_roped, gated = signal("y_ready", 4), signal("q_roped", 1), signal("gated", KD, 2)
    qlat_p, qlat_ev, qrs_ready = signal("qlat_p", 1), signal("qlat_ev", 1), signal("qrs_ready", 1)
    q_asm, k_asm, v_asm = signal("q_asm", NH), signal("k_asm", NH), signal("v_asm", NH)
    qk, smax, expd, normed = signal("qk", 4 * NH), signal("smax", 4 * NH), signal("expd", 4 * NH), signal("normed", NH)
    pt_p, pt_ev, pv, o_done = signal("pt_p", NH), signal("pt_ev", NH, 1), signal("pv", NH), signal("o_done", NH, 1)
    kv_in = [signal("kv_in0", 4 * 16 * (NPG + 1)), signal("kv_in1", 4 * 16 * (NPG + 1))]
    wuv_in, qst_ready = signal("wuv_in", 16), signal("qst_ready", NB)
    kt_p, kt_d, kt_a = signal("kt_p", 4 * NB), signal("kt_d", 4 * NB, 1), signal("kt_a", 4 * NB, 1)
    s_p, s_d, s_a = signal("s_p", 5 * NB), signal("s_d", 5 * NB), signal("s_a", 5 * NB, 1)
    s_max, s_exp = signal("s_max", NB), signal("s_exp", NB)
    spt_p, spt_a, spt_d = signal("spt_p", 5 * NB), signal("spt_a", 2 * NB), signal("spt_d", 3 * NB, 1)
    spv, so_d, so_T, so_a = signal("spv", NB, 2), signal("so_d", NB), signal("so_T", NB), signal("so_a", NB, 1)
    uvs, mixed, x_mid = signal("uvs", 1), signal("mixed", 1), signal("x_mid", 1)
    t0, zconv, silud, prod = signal("t0", 44), signal("zconv", 44, 2), signal("silud", KF), signal("prod", KF)
    act_hi_done, act_ready = signal("act_hi_done", KF), signal("act_ready", KF, 1)
    cl_T, cl_ev = signal("cl_T", 11), signal("cl_ev", 11, 1)
    cl_out = [signal("cl_out0", 32 * 6), signal("cl_out1", 32 * 5)]
    x_new = signal("x_new", 1, 1)

    passed = [nc.alloc_semaphore(f"passed_{e}") for e in ("sp", "act", "dve", "pe", "pool")]

    def two(ap):
        return ap.rearrange("p (a b) -> p a b", a=2)

    def bank_pair(j):
        return PS[:, 2 * (j % 2):2 * (j % 2) + 2, 0:HT]

    with nc.Block() as block:

        @block.sync
        def _(sp):
            sp.dma_start(rows_in[:, 0:4, :], A["x_prompt"][0].rearrange("(n p) d -> p n d", p=128)).then_inc(x_in.sem, 16)
            sp.dma_start(rows_in[0:TS, 4, :], A["x_sample"].rearrange("b s d -> (b s) d")).then_inc(x_in.sem, 16)
            for dst, src in ((ident, "ident"), (ones, "ones"), (causal, "causal"), (causal_s, "causal_s"),
                             (fold, "fold")):
                sp.dma_start(dst[:], A[src]).then_inc(const_in.sem, 16)
            sp.dma_start(ramp[:].rearrange("p a b -> p (a b)"), A["ramp"]).then_inc(const_in.sem, 16)
            sp.dma_start(c_rows[0:1, :], A["c_prompt"]).then_inc(const_in.sem, 16)
            sp.dma_start(c_rows[1:NC, :], A["c_sample"]).then_inc(const_in.sem, 16)
            sp.dma_start(gf_rows[:], A["g_final"].rearrange("(n p) -> n p", p=128)).then_inc(const_in.sem, 16)
            sp.dma_start(tab[:], A["page_table"].rearrange("b n -> (b n)").rearrange("(o n) -> o n", o=1)).then_inc(tab_in.sem, 16)

            def unit(l, u, slot, dst, src):
                sp.wait_ge(lo_ready.sem, lo_ready.at(l, u - 1))
                sp.dma_start(dst, src).then_inc(loaded[slot].sem, 16)

            def square(l, w, u0, n, col0):
                with sp.Fori(0, n // 2) as i:
                    for s in range(2):
                        unit(l, u0 + 2 * i + s, s, raw[:, s].rearrange("p (k n) -> p k n", k=8),
                             w[bass.ds(l, 1), :, bass.ds(col0 + 256 * i + 128 * s, 128)]
                             .rearrange("a (k p) n -> p (a k) n", p=128))

            sp.wait_ge(tab_in.sem, 16)
            with sp.Fori(0, DEPTH) as l:
                sp.wait_ge(x_new.sem, x_new.at(l, 0))
                for r, (name, n) in zip((P_GA, P_GF, P_PS, P_BA, P_GQ, P_GK), (("g_attn", 8), ("g_ffn", 8), ("pool_scale", 8), ("b_ada", 48), ("g_q", 6), ("g_kv", 2))):
                    sp.dma_start(rows[r:r + n, 0, :], A[name][bass.ds(l, 1)].rearrange("a (n p) -> (a n) p", p=128)).then_inc(par_in.sem, 16)
                wc = A["w_conv"][bass.ds(l, 1)].rearrange("a c (n p) -> (a c n) p", p=128)
                sp.dma_start(rows[0:88, 1, :], wc[0:88]).then_inc(par_in.sem, 16)
                sp.dma_start(rows[0:44, 2, :], wc[88:132]).then_inc(par_in.sem, 16)
                sp.dma_start(rows[44:88, 2, :], A["b_conv"][bass.ds(l, 1)].rearrange("a (n p) -> (a n) p", p=128)).then_inc(par_in.sem, 16)
                scv = A["state_conv"][bass.ds(l, 1)].rearrange("a b r (n p) -> (a b r n) p", p=128)
                sp.dma_start(rows[:, 3:8, :], scv[0:640].rearrange("(c r) p -> r c p", r=128)).then_inc(par_in.sem, 16)
                sp.dma_start(rows[0:64, 8, :], scv[640:704]).then_inc(par_in.sem, 16)
                spl = A["state_pool"][bass.ds(l, 1)].rearrange("a b r (n p) -> (a b r n) p", p=128)
                sp.dma_start(rows[:, 9:16, :], spl[0:896].rearrange("(c r) p -> r c p", r=128)).then_inc(par_in.sem, 16)
                sp.dma_start(rows[0:64, 16, :], spl[896:960]).then_inc(par_in.sem, 16)
                sp.dma_start(rope[:].rearrange("p a b -> p (a b)"), A["rope"]).then_inc(rope_in.sem, 16)
                square(l, A["w_ada"], U_ADA, 48, 0)
                square(l, A["w_in"], U_CQ, 8, 0)
                for s in range(2):
                    unit(l, U_KR + s, s, raw[:, s, 0:128].rearrange("p (k n) -> p k n", k=4),
                         A["w_in"][bass.ds(l, 1), 512 * s:512 * s + 512, C_KR:C_KR + DR].rearrange("a (k p) n -> p (a k) n", p=128))
                square(l, A["w_in"], U_U, 8, C_U)
                w_uq = A["w_uq"].rearrange("a (k p) (h n) -> p a k h n", p=128, n=DN + DR)
                with sp.Fori(0, 4) as i:
                    for s in range(2):
                        dst = raw[:, s, 0:768].rearrange("p (k h n) -> p k h n", k=KQ, h=2)
                        sp.wait_ge(lo_ready.sem, lo_ready.at(l, U_QN + 2 * i + s - 1))
                        for j in range(2):
                            sp.dma_start(dst[:, :, j, :], w_uq[:, bass.ds(l, 1), :, bass.ds(4 * i + 2 * s + j, 1), 0:DN]
                                         .rearrange("p a k h n -> p (a k) (h n)")).then_inc(loaded[s].sem, 16)
                with sp.Fori(0, 2) as i:
                    for s in range(2):
                        dst = raw[:, s, 0:768].rearrange("p (k h n) -> p k h n", k=KQ, h=4)
                        sp.wait_ge(lo_ready.sem, lo_ready.at(l, U_QR + 2 * i + s - 1))
                        for j in range(4):
                            sp.dma_start(dst[:, :, j, :], w_uq[:, bass.ds(l, 1), :, bass.ds(8 * i + 4 * s + j, 1), DN:DN + DR]
                                         .rearrange("p a k h n -> p (a k) (h n)")).then_inc(loaded[s].sem, 16)
                for s in range(2):
                    unit(l, U_POOL + s, s, raw[:, s].rearrange("p (k n) -> p k n", k=4),
                         A["w_pool"][bass.ds(l, 1), 2 * s:2 * s + 2].rearrange("a g (k p) n -> p (a g k) n", p=128))
                square(l, A["w_in"], U_G, 16, C_G)
                for w, u0 in ((A["w_uk"], U_UK), (A["w_uv"], U_UV)):
                    for s in range(2):
                        unit(l, u0 + s, s, raw[:, s].rearrange("p (k n) -> p k n", k=2),
                             w[bass.ds(l, 1)].rearrange("a (k p) h n -> p (a k) (h n)", p=128)[:, :, 512 * s:512 * s + 512])
                wo = A["w_out"]
                for s in range(2):
                    unit(l, U_OUT + s, s, raw[:, s].rearrange("p (k n) -> p k n", k=8),
                         wo[bass.ds(l, 1), :, 128 * s:128 * s + 128].rearrange("a (k p) n -> p (a k) n", p=128))
                sp.wait_ge(o_done.sem, o_done.at(l, NH))
                sp.dma_start(wuv[:], A["w_uv"][bass.ds(l, 1)].rearrange("a (k p) h n -> p (a k) (h n)", p=128)).then_inc(wuv_in.sem, 16)
                sp.wait_ge(lat_out.sem, lat_out.at(l, 32))
                sp.sem_inc(passed[0], 1)
                with sp.Fori(0, NB // 2) as i:
                    for s in range(2):
                        sp.wait_ge(spv.sem, spv.at(l, 2 * i + s - 1))
                        sp.dma_start(newk[:, s, :], O["lat_s"][bass.ds(l, 1), bass.ds(2 * i + s, 1)].rearrange("a b s c -> (a b s) c")).then_inc(kv_in[s].sem, 16)
                        for j in range(NPG):
                            page = sp.value_load(tab[0:1, bass.ds((2 * i + s) * NPG + j, 1)], min_val=0, max_val=A["cache_latent"].shape[1] - 1)
                            sp.dma_start(pages[s][:, j, :], A["cache_latent"][bass.ds(l, 1), bass.ds(page, 1)].rearrange("a b k c -> (a b k) c")).then_inc(kv_in[s].sem, 16)
                with sp.Fori(1, 4) as i:
                    for s in range(2):
                        unit(l, U_OUT + 2 * i + s, s, raw[:, s].rearrange("p (k n) -> p k n", k=8),
                             wo[bass.ds(l, 1), :, bass.ds(256 * i + 128 * s, 128)].rearrange("a (k p) n -> p (a k) n", p=128))
                with sp.Fori(0, KF) as j:
                    for s in range(2):
                        unit(l, U_UP + 2 * j + s, s, raw[:, s].rearrange("p (k n) -> p k n", k=8),
                             A["w_up"][bass.ds(l, 1), :, bass.ds(DF * s + 128 * j, 128)].rearrange("a (k p) n -> p (a k) n", p=128))
                with sp.Fori(0, 4) as i:
                    for v in range(6):
                        kk = 8 if v % 3 < 2 else KF - 16
                        r0 = 1024 * (v % 3)
                        unit(l, U_DOWN + 6 * i + v, v % 2, raw[:, v % 2, 0:128 * kk].rearrange("p (k n) -> p k n", k=kk),
                             A["w_down"][bass.ds(l, 1), r0:r0 + 128 * kk, bass.ds(256 * i + 128 * (v // 3), 128)]
                             .rearrange("a (k p) n -> p (a k) n", p=128))

        @block.scalar
        def _(act):
            def hi(l, u, i, slot):
                pieces = loads_before(u + 4) - loads_before(u + 2) if not isinstance(i, int) else 0
                act.wait_ge(loaded[slot].sem, 16 * (l * LOADS + loads_before(u + 2) + pieces * i))
                act.wait_ge(unit_used.sem, unit_used.at(l, u + 2 * i - 1))
                nc.scalar.activation(whi[:, slot], raw[:, slot], ACT.Copy).then_inc(hi_ready.sem, 1)

            for phase in ("qkv", "u", "uq", "g", "uk", "uv", "up"):
                act.sem_inc(free[phase].sem, 2)
            for readout in (pt_ev, kt_a, s_a, so_a, cl_ev):
                act.sem_inc(readout.sem, 1)
            for f in range(KD):
                act.wait_ge(start_T.sem, f + 1)
                b = 2 * (f % 2)
                nc.scalar.activation(x[:, f, 0:TP], PS[:, b, 0:TP], ACT.Copy)
                nc.scalar.activation(x[:, f, TP:T], PS[:, b + 1, 0:TS], ACT.Copy).then_inc(start_ev.sem, 1)
            act.wait_ge(start_T.sem, KD + 1)
            nc.scalar.activation(cT[:].rearrange("p a b -> p (a b)"), PS[:, 4, 0:KD * NC], ACT.Copy)
            nc.scalar.activation(g_fin[:], PS[:, 4, 128:128 + KD], ACT.Copy)
            nc.scalar.activation(ident_r[:], ident[:], ACT.Copy)
            nc.scalar.drain()
            nc.scalar.activation(cond[:, :, 0:NC], cT[:], ACT.Copy).then_inc(cond_hi.sem, 1)
            act.wait_ge(eps_set.sem, 1)

            def norm_squares(l, k):
                with act.Fori(0, KD // 2) as i:
                    for s in range(2):
                        act.wait_ge(sq_used.sem, sq_used.at(l, KD * k + 2 * i + s - 1))
                        nc.scalar.activation(tmp[:, s, :], x[:, bass.ds(2 * i + s, 1), :].rearrange("p a b -> p (a b)"), ACT.Square).then_inc(sq.sem, 1)

            def root_of(l, k, n):
                act.wait_ge(ssum_p.sem, ssum_p.at(l, k + 1))
                nc.scalar.activation(two(kv_sum[:, 1, :] if k == 2 else rinv[:]), PS[:, 6:8, 0:HT], ACT.Sqrt, bias=eps[:, 0:1], scale=1.0 / n).then_inc(root.sem, 1)

            def norm_affine(l, k, gain, shift):
                with act.Fori(0, KD // 2) as i:
                    for s in range(2):
                        act.wait_ge(scaled.sem, scaled.at(l, KD * k + 2 * i + s + 1))
                        nc.scalar.activation(tmp[:, s, 0:TP], tmp[:, s, 0:TP], ACT.Identity,
                                             bias=mod[:, bass.ds(shift + 2 * i + s, 1), 0:1].rearrange("p a b -> p (a b)"),
                                             scale=gain[:, bass.ds(2 * i + s, 1), 0:1].rearrange("p a b -> p (a b)"))
                        nc.scalar.drain()
                        nc.scalar.activation(h_hi[:, bass.ds(2 * i + s, 1), :].rearrange("p a b -> p (a b)"), tmp[:, s, :], ACT.Copy).then_inc(affine.sem, 1)

            def tiles(l, u0, n, evac):
                def pair(i):
                    for s in range(2):
                        hi(l, u0 + s + 1 + (2 * i if isinstance(i, int) else 0), 0 if isinstance(i, int) else i, (s + 1) % 2)
                        act.wait_ge(unit_used.sem, unit_used.at(l, 2 * i + (u0 + s + 1)))
                        evac(2 * i + s, s)

                if n > 2:
                    with act.Fori(0, n // 2 - 1) as i:
                        pair(i)
                pair(n // 2 - 1)

            def only_units(l, u0, n):
                with act.Fori(0, n // 2 - 1) as i:
                    hi(l, u0 + 1, i, 1)
                    hi(l, u0 + 2, i, 0)
                hi(l, u0 + n - 1, 0, 1)
                hi(l, u0 + n, 0, 0)

            def tile_of(t, f):
                return two(t[:, bass.ds(f, 1), :].rearrange("p a b -> p (a b)"))

            with act.Fori(0, DEPTH) as l:
                hi(l, 0, 0, 0)
                act.wait_ge(par_T.sem, par_T.at(l, 1))
                nc.scalar.activation(par[:], PS[:, 4, 0:P_ALL], ACT.Copy)
                nc.scalar.activation(convp[:].rearrange("p a b -> p (a b)"), PS[:, 4, 80:256], ACT.Copy)
                cp = conv_prev[:].rearrange("p a b -> p (a b)")
                nc.scalar.activation(cp[:, 0:512], PS[:, 5, :], ACT.Copy)
                nc.scalar.activation(cp[:, 512:704], PS[:, 4, 256:448], ACT.Copy)
                pp = pool_prev[:].rearrange("p a b -> p (a b)")
                nc.scalar.activation(pp[:, 0:512], PS[:, 6, :], ACT.Copy)
                nc.scalar.activation(pp[:, 512:960], PS[:, 7, 0:448], ACT.Copy).then_inc(par_ev.sem, 1)
                only_units(l, U_ADA, 48)
                norm_squares(l, 0)
                root_of(l, 0, D)
                norm_affine(l, 0, gain1, 0)


                def to_cq(f, s):
                    nc.scalar.activation(tile_of(cq, f), bank_pair(s), ACT.Copy).then_inc(free["qkv"].sem, 1)

                def to_ckv(f, s):
                    nc.scalar.activation(tile_of(ckv, f), bank_pair(s), ACT.Copy).then_inc(free["qkv"].sem, 1)

                tiles(l, U_CQ, 6, to_cq)
                tiles(l, U_KV, 2, to_ckv)
                hi(l, U_KR + 1, 0, 1)
                hi(l, U_KR + 2, 0, 0)
                act.wait_ge(unit_used.sem, unit_used.at(l, U_KR + 2))
                nc.scalar.activation(two(krope[:]), PS[0:DR, 0:2, 0:HT], ACT.Copy).then_inc(free["qkv"].sem, 2)


                def to_u(f, s):
                    b = 2 * s
                    ue = uext[:, bass.ds(f, 1), :].rearrange("p a b -> p (a b)")
                    nc.scalar.activation(ue[:, CTX:CTX + HT], PS[:, b, 0:HT], ACT.Copy)
                    nc.scalar.activation(ue[:, CTX + HT:US], PS[:, b + 1, 0:TP - HT], ACT.Copy)
                    nc.scalar.activation(ue[:, US:UE].rearrange("p (b c) -> p b c", b=NB)[:, :, CTX:], PS[:, b + 1, TP - HT:HT].rearrange("p (b c) -> p b c", b=NB),
                                         ACT.Copy).then_inc(free["u"].sem, 1)

                tiles(l, U_U, 4, to_u)
                root_of(l, 1, QL)
                root_of(l, 2, KVL)
                tiles(l, U_U + 4, 4, lambda f, s: to_u(f + 4, s))
                act.wait_ge(last_T.sem, last_T.at(l, 1))
                nc.scalar.activation(pool_rows[0:120, 0], PS[0:120, 4:6, :], ACT.Copy)
                nc.scalar.activation(pool_rows[0:CTX, 1], PS[0:CTX, 6:8, :], ACT.Copy).then_inc(last_ev.sem, 1)
                act.wait_ge(last_ev.sem, last_ev.at(l, 1))
                act.dma_start(O["pool_s"][bass.ds(l, 1)].rearrange("a b r d -> (a b r) d"), pool_rows[0:120, 0].rearrange("p a b -> p (a b)")).then_inc(last_out.sem, 16)
                act.dma_start(O["pool_p"][bass.ds(l, 1)].rearrange("a b r d -> (a b r) d"), pool_rows[0:CTX, 1].rearrange("p a b -> p (a b)")).then_inc(last_out.sem, 16)
                for n in range(5):
                    act.wait_ge(lat_T.sem, lat_T.at(l, n + 1))
                    m = 128 if n < 4 else TS
                    nc.scalar.activation(lat_rows[0:m, n, :], PS[0:m, 4 + n % 2, 0:LAT], ACT.Copy).then_inc(lat_ev.sem, 1)
                act.wait_ge(lat_ev.sem, lat_ev.at(l, 5))
                act.dma_start(O["lat_p"][bass.ds(l, 1)].rearrange("a b (n p) c -> p (a b n) c", p=128), lat_rows[:, 0:4, :]).then_inc(lat_out.sem, 16)
                act.dma_start(O["lat_s"][bass.ds(l, 1)].rearrange("a b s c -> (a b s) c"), lat_rows[0:TS, 4, :]).then_inc(lat_out.sem, 16)

                act.wait_ge(last_out.sem, last_out.at(l, 32))
                act.wait_ge(lat_out.sem, lat_out.at(l, 32))

                def to_qn(f, s):
                    nc.scalar.activation(tile_of(qn, f), bank_pair(s), ACT.Copy).then_inc(free["uq"].sem, 1)

                def to_qr(f, s):
                    nc.scalar.activation(tile_of(qr, f), bank_pair(s), ACT.Copy).then_inc(free["uq"].sem, 1)

                tiles(l, U_QN, 8, to_qn)
                tiles(l, U_QR, 4, to_qr)
                hi(l, U_POOL + 1, 0, 1)
                hi(l, U_POOL + 2, 0, 0)

                act.wait_ge(free["pool"].sem, free["pool"].at(l, 8))

                def to_gate_a(f, s):
                    act.wait_ge(gated.sem, gated.at(l, f - 1))
                    nc.scalar.activation(two(tmp[:, s, :]), bank_pair(s), ACT.Sigmoid).then_inc(free["g"].sem, 1)

                def to_gate_b(f, s):
                    nc.scalar.activation(tile_of(gate_b, f), bank_pair(s), ACT.Sigmoid).then_inc(free["g"].sem, 1)

                tiles(l, U_G, 8, to_gate_a)
                tiles(l, U_G + 8, 8, to_gate_b)

                for p in range(8):
                    if p % 4 == 0:
                        hi(l, U_UK + p // 4 + 1, 0, (p // 4 + 1) % 2)
                    act.wait_ge(full["uk"].sem, full["uk"].at(l, p + 1))
                    nc.scalar.activation(kn[:, p, :], PS[:, 2 * (p % 2), :], ACT.Copy)
                    nc.scalar.activation(wukT[:, p, :], PS[:, 2 * (p % 2) + 1, 0:KVL], ACT.Copy).then_inc(free["uk"].sem, 1)
                for n in range(4):
                    if n % 2 == 0:
                        hi(l, U_UV + n // 2 + 1, 0, (n // 2 + 1) % 2)
                    act.wait_ge(full["uv"].sem, full["uv"].at(l, n + 1))
                    nc.scalar.activation(vn[:, 2 * (n % 2):2 * (n % 2) + 2, 512 * (n // 2):512 * (n // 2) + 512], PS[:, 2 * (n % 2):2 * (n % 2) + 2, :], ACT.Copy).then_inc(free["uv"].sem, 1)
                act.wait_ge(qlat_p.sem, qlat_p.at(l, 1))
                for c in range(KC):
                    for g in range(2):
                        for h8 in range(8):
                            last = nc.scalar.activation(qlat[:, c, :, 2 * h8 + g, :], PS[:, 4 + 2 * c + g, 64 * h8:64 * h8 + 64].rearrange("p (b s) -> p b s", b=NB), ACT.Copy)

                last.then_inc(qlat_ev.sem, 1)

                def prompt_head(i, j):
                    h = 4 * i + j
                    for qb in range(4):
                        act.wait_ge(smax.sem, smax.at(l, 4 * h + qb + 1))
                        o = 64 * qb * (qb + 1)
                        nc.scalar.activation(prob[:, o:o + 128 * (qb + 1)], PS[:, qb, 0:128 * (qb + 1)], ACT.Exp,
                                             bias=softm[:, 4 + qb:5 + qb], scale=SCALE, accum_out=softm[:, 8 + qb:9 + qb]).then_inc(expd.sem, 1)
                    act.wait_ge(pt_p.sem, pt_p.at(l, h + 1))
                    nc.scalar.activation(probT[:, 0:512], PS[:, 4, :], ACT.Copy)
                    nc.scalar.activation(probT[:, 512:896], PS[:, 5, 0:384], ACT.Copy)
                    nc.scalar.activation(probT[:, 896:1280], PS[:, 6, 0:384], ACT.Copy).then_inc(pt_ev.sem, 1)

                def head_query(p, s):
                    nc.scalar.activation(q96[0:DN, s, :], qn[64 * s:64 * s + 64, bass.ds(p, 1), 0:TP].rearrange("p a b -> p (a b)"),
                                         ACT.Copy).then_inc(q_asm.sem, 1)

                head_query(0, 0)
                head_query(0, 1)
                with act.Fori(0, 3) as i:
                    for j in range(4):
                        prompt_head(i, j)
                        head_query(2 * i + (j // 2 + 1), j % 2)
                for j in range(4):
                    prompt_head(3, j)
                    if j < 2:
                        head_query(7, j)

                with act.Fori(0, NB // 2) as i:
                    for s in range(2):
                        b = 2 * i + s

                        def keys(g):
                            act.wait_ge(kt_p.sem, kt_p.at(l, 4 * b + g + 1))
                            nc.scalar.activation(keysT[g % 2][:, 1, :], PS[:, 1, :], ACT.Copy).then_inc(kt_a.sem, 1)

                        def scores(g):
                            act.wait_ge(s_d.sem, s_d.at(l, 5 * b + g + 1))
                            w = 512 if g < 4 else NS
                            nc.scalar.activation(sc[:, 512 * g:512 * g + w], PS[:, 3 + g % 2, 0:w], ACT.Copy).then_inc(s_a.sem, 1)

                        keys(0)
                        for g in range(4):
                            if g < 3:
                                keys(g + 1)
                            scores(g)
                        scores(4)
                        nc.scalar.drain()
                        act.wait_ge(s_max.sem, s_max.at(l, b + 1))
                        nc.scalar.activation(sc[:], sc[:], ACT.Exp, bias=softm[:, 24:25], scale=SCALE, accum_out=softm[:, 25:26]).then_inc(s_exp.sem, 1)
                        for g in (0, 2):
                            act.wait_ge(spt_p.sem, spt_p.at(l, 5 * b + g + 1))
                            nc.scalar.activation(pT[:, 4 * g:4 * g + 4, :].rearrange("p a b -> p (a b)"), PS[:, 5 + g % 2, :], ACT.Copy).then_inc(spt_a.sem, 1)
                        act.wait_ge(so_T.sem, so_T.at(l, b + 1))
                        for c in range(KC):
                            last = nc.scalar.activation(olatT[:, c, :, bass.ds(b, 1), :].rearrange("p h b s -> p h (b s)"),
                                                        PS[:, 7, 256 + 128 * c:384 + 128 * c].rearrange("p (h s) -> p h s", h=NH), ACT.Copy)
                        last.then_inc(so_a.sem, 1)

                only_units(l, U_OUT, 8)
                act.wait_ge(x_mid.sem, x_mid.at(l, 1))
                act.sem_inc(passed[1], 1)
                norm_squares(l, 1)
                root_of(l, 3, D)
                norm_affine(l, 1, gain2, 24)

                def up_pair(j):
                    for s in range(2):
                        b = 2 * s
                        f = j + KF * s
                        if isinstance(j, int):
                            hi(l, U_UP + 2 * j + s + 1, 0, (s + 1) % 2)
                        else:
                            hi(l, U_UP + s + 1, j, (s + 1) % 2)
                        nc.scalar.drain()
                        act.wait_ge(unit_used.sem, unit_used.at(l, 2 * j + (U_UP + s + 1)))
                        act.wait_ge(zconv.sem, zconv.at(l, 2 * j + (s - 1)))
                        zs = zext[:, s, ZS:ZE].rearrange("p (b c) -> p b c", b=NB)
                        nc.scalar.activation(zext[:, s, 2:2 + HT], PS[:, b, 0:HT], ACT.Copy)
                        nc.scalar.activation(zext[:, s, 2 + HT:ZS], PS[:, b + 1, 0:TP - HT], ACT.Copy)
                        nc.scalar.activation(zs[:, :, 2:], PS[:, b + 1, TP - HT:HT].rearrange("p (b c) -> p b c", b=NB), ACT.Copy).then_inc(free["up"].sem, 1)
                        prev = conv_prev[:, :, bass.ds(f, 1)].rearrange("p (b r) o -> p b (r o)", b=NB)
                        nc.scalar.activation(zs[:, :, 0:2], prev, ACT.Copy)
                        nc.scalar.drain()
                        cl = conv_last[:, bass.ds(f, 1), :].rearrange("p a b -> p (a b)")
                        nc.scalar.activation(cl[:, 0:2], zext[:, s, TP:ZS], ACT.Copy)
                        nc.scalar.activation(cl[:, 2:].rearrange("p (b r) -> p b r", b=NB), zs[:, :, NS:], ACT.Copy)
                        act.wait_ge(act_ready.sem, act_ready.at(l, j))
                        nc.scalar.activation(conv[:, s, 0:ZE - 2], zext[:, s, 2:ZE], ACT.Identity,
                                             bias=convp[:, 1, bass.ds(2 * KF + f, 1)], scale=convp[:, 1, bass.ds(f, 1)]).then_inc(t0.sem, 1)
                    act.wait_ge(zconv.sem, zconv.at(l, 2 * j + 1))
                    nc.scalar.activation(conv[:, 0, 0:ZE - 2], conv[:, 0, 0:ZE - 2], ACT.Silu).then_inc(silud.sem, 1)
                    act.wait_ge(prod.sem, prod.at(l, j + 1))
                    ah = act_hi[:, bass.ds(j, 1), :].rearrange("p a b -> p (a b)")
                    nc.scalar.activation(ah[:, 0:TP], conv[:, 0, 0:TP], ACT.Copy)
                    nc.scalar.activation(ah[:, TP:T].rearrange("p (b c) -> p b c", b=NB), conv[:, 0, ZS:ZE].rearrange("p (b c) -> p b c", b=NB)[:, :, 0:NS],
                                         ACT.Copy).then_inc(act_hi_done.sem, 1)

                with act.Fori(0, KF - 1) as j:
                    up_pair(j)
                up_pair(KF - 1)
                def state_rows(n):
                    act.wait_ge(cl_T.sem, cl_T.at(l, n + 1))
                    if n >= 2:
                        act.wait_ge(cl_out[n % 2].sem, cl_out[n % 2].at(l, 32 * (n // 2)))
                    nc.scalar.activation(conv_rows[:, n % 2, :], PS[0:2 * NC, 4 + n % 2, :], ACT.Copy).then_inc(cl_ev.sem, 1)
                    act.wait_ge(cl_ev.sem, cl_ev.at(l, n + 1))
                    act.dma_start(O["conv_p"][bass.ds(l, 1), :, :, 512 * n:512 * n + 512].rearrange("a b r d -> (a b r) d"), conv_rows[0:2, n % 2, :]).then_inc(cl_out[n % 2].sem, 16)
                    act.dma_start(O["conv_s"][bass.ds(l, 1), :, :, 512 * n:512 * n + 512].rearrange("a b r d -> (a b r) d"), conv_rows[2:2 * NC, n % 2, :]).then_inc(cl_out[n % 2].sem, 16)

                hi(l, U_DOWN + 1, 0, 1)
                for n in range(11):
                    state_rows(n)
                with act.Fori(0, 11) as i:
                    hi(l, U_DOWN + 2, i, 0)
                    hi(l, U_DOWN + 3, i, 1)
                for s in range(2):
                    act.wait_ge(cl_out[s].sem, cl_out[s].at(l + 1, 0))
                    act.sem_inc(passed[1], 1)

            with act.Fori(0, KD // 2) as i:
                for s in range(2):
                    act.wait_ge(sq_used.sem, sq_used.at(DEPTH, 2 * i + s - 1))
                    nc.scalar.activation(tmp[:, s, :], x[:, bass.ds(2 * i + s, 1), :].rearrange("p a b -> p (a b)"), ACT.Square).then_inc(sq.sem, 1)
            root_of(DEPTH, 0, D)
            for n in range(5):
                m = 128 if n < 4 else TS
                act.wait_ge(fin_T.sem, n + 1)
                if n >= 2:
                    act.wait_ge(y_out[n % 2].sem, 16 * (n // 2))
                nc.scalar.activation(y_rows[0:m, n % 2, :].rearrange("p (a b) -> p a b", a=2), PS[0:m, 2 * (n % 2):2 * (n % 2) + 2, :], ACT.Copy).then_inc(fin_ev.sem, 1)
                act.wait_ge(fin_ev.sem, n + 1)
                dst = O["y_p"][0, 128 * n:128 * n + 128, :] if n < 4 else O["y_s"].rearrange("b s d -> (b s) d")
                act.dma_start(dst, y_rows[0:m, n % 2, :]).then_inc(y_out[n % 2].sem, 16)
            act.wait_ge(y_out[0].sem, 48)
            act.wait_ge(y_out[1].sem, 32)
            act.wait_ge(lat_out.sem, lat_out.at(DEPTH, 0))
            act.wait_ge(last_out.sem, last_out.at(DEPTH, 0))

        @block.gpsimd
        def _(pool):
            pool.sem_inc(lo_ready.sem, 2)

            def lo(l, u, slot):
                pool.wait_ge(hi_ready.sem, hi_ready.at(l, u + 1))
                nc.gpsimd.tensor_tensor(wlo[:, slot], raw[:, slot], whi[:, slot].bitcast(F32), ALU.subtract).then_inc(lo_ready.sem, 1)

            def head_parts(p, s, j):
                pool.sem_inc(passed[4], 1)
                nc.gpsimd.tensor_copy(q96[DN:96, s, :], qr[32 * j:32 * j + 32, bass.ds(p[0], 1), 0:TP].rearrange("p a b -> p (a b)"))
                nc.gpsimd.drain()
                nc.gpsimd.tensor_copy(k96[0:DN, s, :], kn[64 * s:64 * s + 64, bass.ds(p[1], 1), :].rearrange("p a b -> p (a b)")).then_inc(k_asm.sem, 1)

            with pool.Fori(0, DEPTH) as l:
                with pool.Fori(0, U_OUT // 2) as i:
                    lo(l, 2 * i, 0)
                    lo(l, 2 * i + 1, 1)
                lo(l, U_OUT, 0)
                nc.gpsimd.drain()
                pool.wait_ge(free["uv"].sem, free["uv"].at(l, 4))
                pool.wait_ge(q_roped.sem, q_roped.at(l, 1))
                head_parts((0, 0), 0, 0)
                nc.gpsimd.drain()
                head_parts((0, 0), 1, 1)
                with pool.Fori(0, 3) as i:
                    for j in range(4):
                        nc.gpsimd.drain()
                        pool.wait_ge(qk.sem, qk.at(l, 16 * i + (4 * j + 4)))
                        head_parts((i + (j + 2) // 4, 2 * i + (j // 2 + 1)), j % 2, (j + 2) % 4)
                for j in range(2):
                    nc.gpsimd.drain()
                    pool.wait_ge(qk.sem, qk.at(l, 4 * (12 + j) + 4))
                    head_parts((3, 7), j, j + 2)
                nc.gpsimd.drain()
                with pool.Fori(0, (UNITS - U_OUT - 2) // 2) as i:
                    lo(l, U_OUT + 1 + 2 * i, 1)
                    lo(l, U_OUT + 2 + 2 * i, 0)
                lo(l, UNITS - 1, 1)

        @block.vector
        def _(dve):
            v = nc.vector

            def flat(ap):
                return ap.rearrange("p a b -> p (a b)")

            def by_seq(ap):
                return ap.rearrange("p (b c) -> p b c", b=NB)

            def over_tokens(ap):
                return ap.unsqueeze(2).broadcast_to([128, NB, NS])

            v.memset(eps[:], EPS).then_inc(eps_set.sem, 1)
            for g in (sq_used, gated, zconv, free["pool"], free["out"], free["down"]):
                dve.sem_inc(g.sem, 2)
            for readout in (o_done, kt_d, spt_d, act_ready, x_new):
                dve.sem_inc(readout.sem, 1)
            dve.wait_ge(cond_hi.sem, 1)
            v.tensor_tensor(cond[:, :, NC:2 * NC], cT[:], cond[:, :, 0:NC].bitcast(F32), ALU.subtract).then_inc(cond_ready.sem, 1)

            def sum_squares(l, k, n):
                dve.wait_ge(sq.sem, sq.at(l, KD * k + 1))
                v.tensor_copy(sumsq[:], tmp[:, 0, :]).then_inc(sq_used.sem, 1)

                def add(f, s):
                    v.drain()
                    dve.wait_ge(sq.sem, sq.at(l, f + (KD * k + 1)))
                    v.tensor_tensor(sumsq[:], sumsq[:], tmp[:, s, :], ALU.add).then_inc(sq_used.sem, 1)

                add(1, 1)
                with dve.Fori(1, KD // 2) as i:
                    add(2 * i, 0)
                    add(2 * i + 1, 1)
                v.drain().then_inc(ssum.sem, 1)

            def norm(l, k, sums, gain, shift):
                sum_squares(l, k, D)
                dve.wait_ge(root.sem, root.at(l, sums + 1))
                v.reciprocal(rinv[:], rinv[:])
                v.drain()

                def scale(f, s):
                    v.tensor_tensor(tmp[:, s, :], flat(x[:, bass.ds(f, 1), :]), rinv[:], ALU.mult)
                    v.drain()
                    t = by_seq(tmp[:, s, TP:T])
                    v.tensor_tensor(t, t, over_tokens(flat(gain[:, bass.ds(f, 1), 1:NC])), ALU.mult)
                    v.drain()
                    v.tensor_tensor(t, t, over_tokens(flat(mod[:, bass.ds(f + shift, 1), 1:NC])), ALU.add).then_inc(scaled.sem, 1)

                def rest(f, s):
                    dve.wait_ge(affine.sem, affine.at(l, f + (KD * k + 1)))
                    v.tensor_tensor(flat(h_lo[:, bass.ds(f, 1), :]), tmp[:, s, :], flat(h_hi[:, bass.ds(f, 1), :]).bitcast(F32), ALU.subtract)
                    v.drain()

                scale(0, 0)
                with dve.Fori(0, KD // 2 - 1) as i:
                    scale(2 * i + 1, 1)
                    rest(2 * i, 0)
                    scale(2 * i + 2, 0)
                    rest(2 * i + 1, 1)
                scale(KD - 1, 1)
                rest(KD - 2, 0)
                rest(KD - 1, 1)

            def residual(l, phase, gate, u0, units):
                def tile(m, s):
                    dve.wait_ge(unit_used.sem, unit_used.at(l, u0 + units * (m + 1)))
                    xm = flat(x[:, bass.ds(m, 1), :])
                    g = mod[:, bass.ds(m + gate, 1), :].rearrange("p a b -> p (a b)")
                    gated_s = sumsq[:, TS * s:TS * s + TS]
                    t = by_seq(gated_s)
                    v.scalar_tensor_tensor(xm[:, 0:HT], PS[:, 2 * s, 0:HT], g[:, 0:1], xm[:, 0:HT], ALU.mult, ALU.add)
                    v.scalar_tensor_tensor(xm[:, HT:TP], PS[:, 2 * s + 1, 0:TP - HT], g[:, 0:1], xm[:, HT:TP], ALU.mult, ALU.add)
                    v.tensor_tensor(t, by_seq(PS[:, 2 * s + 1, TP - HT:HT]), over_tokens(g[:, 1:NC]), ALU.mult).then_inc(free[phase].sem, 1)
                    v.drain()
                    v.tensor_tensor(xm[:, TP:T], xm[:, TP:T], gated_s, ALU.add)

                with dve.Fori(0, KD // 2) as i:
                    tile(2 * i, 0)
                    tile(2 * i + 1, 1)

            with dve.Fori(0, DEPTH) as l:
                dve.wait_ge(par_ev.sem, par_ev.at(l, 1))
                v.memset(uext[:, :, 0:CTX], 0.0)
                for b in range(NB):
                    o = US + b * (CTX + NS)
                    v.tensor_copy(uext[:, :, o:o + CTX], pool_prev[:, b * CTX:(b + 1) * CTX, :].rearrange("p r f -> p f r"))
                with dve.Fori(0, 24) as i:
                    for s in range(2):
                        dve.wait_ge(unit_used.sem, unit_used.at(l, 2 * i + (s + 1)))
                        dve.wait_ge(ada_T.sem, ada_T.at(l, 2 * i + (s - 1)))
                        v.tensor_copy(ada_rows[:, s, :], PS[0:2 * NC, 4 + s, 0:128]).then_inc(ada_ev.sem, 1)
                dve.wait_ge(ada_T.sem, ada_T.at(l, 48))
                v.tensor_tensor(mod[:], PS[:, 6, 0:48 * NC].rearrange("p (a b) -> p a b", a=48),
                                par[:, P_BA:P_GQ].unsqueeze(2).broadcast_to([128, 48, NC]), ALU.add)
                v.drain()
                v.scalar_tensor_tensor(gain1[:], mod[:, 8:16, :], 1.0, par[:, P_GA:P_GF].unsqueeze(2).broadcast_to([128, KD, NC]), ALU.add, ALU.mult)
                v.scalar_tensor_tensor(gain2[:], mod[:, 32:40, :], 1.0, par[:, P_GF:P_PS].unsqueeze(2).broadcast_to([128, KD, NC]), ALU.add, ALU.mult).then_inc(mod_ready.sem, 1)
                norm(l, 0, 0, gain1, 0)
                v.drain().then_inc(h_ready.sem, 1)

                def latent_squares(src, n, dst, s0):
                    for f in range(n):
                        dve.wait_ge(free["qkv"].sem, free["qkv"].at(l, s0 + f + 1))
                        if f == 0:
                            v.tensor_tensor(dst, src[:, f, :], src[:, f, :], ALU.mult)
                        else:
                            v.tensor_tensor(tmp[:, 0, :], src[:, f, :], src[:, f, :], ALU.mult)
                            v.drain()
                            v.tensor_tensor(dst, dst, tmp[:, 0, :], ALU.add)
                        v.drain()
                    v.drain().then_inc(ssum.sem, 1)

                latent_squares(cq, KQ, sumsq[:], 0)
                latent_squares(ckv, KC, kv_sum[:, 0, :], KQ)
                dve.wait_ge(free["qkv"].sem, free["qkv"].at(l, 10))
                dve.wait_ge(rope_in.sem, rope_in.at(l, 16))
                dve.sem_inc(passed[2], 1)
                half_turn = [(j + 16) % 32 for j in range(32)]
                v.stream_shuffle(tmp[0:DR, 1, :], krope[:], mask=half_turn)
                v.drain()
                v.tensor_tensor(tmp[0:DR, 1, :], tmp[0:DR, 1, :], rope[0:DR, 1, :], ALU.mult)
                v.tensor_tensor(krope[:], krope[:], rope[0:DR, 0, :], ALU.mult)
                v.drain()
                v.tensor_tensor(krope[:], krope[:], tmp[0:DR, 1, :], ALU.add)
                dve.wait_ge(root.sem, root.at(l, 2))
                v.reciprocal(rinv[:], rinv[:])
                v.drain()
                for f in range(KQ):
                    v.scalar_tensor_tensor(cq[:, f, :], cq[:, f, :], par[:, P_GQ + f:P_GQ + f + 1], rinv[:], ALU.mult, ALU.mult)
                    v.drain()
                    v.tensor_copy(cq_hi[:, f, :], cq[:, f, :])
                    v.drain()
                    v.tensor_tensor(cq_lo[:, f, :], cq[:, f, :], cq_hi[:, f, :].bitcast(F32), ALU.subtract)
                v.drain().then_inc(cqn.sem, 1)
                dve.wait_ge(root.sem, root.at(l, 3))
                v.reciprocal(kv_sum[:, 1, :], kv_sum[:, 1, :])
                v.drain()
                for f in range(KC):
                    v.scalar_tensor_tensor(ckv[:, f, :], ckv[:, f, :], par[:, P_GK + f:P_GK + f + 1], kv_sum[:, 1, :], ALU.mult, ALU.mult)
                    v.drain()
                    v.tensor_copy(ckv_hi[:, f, :], ckv[:, f, :])
                    v.drain()
                    v.tensor_tensor(ckv_lo[:, f, :], ckv[:, f, :], ckv_hi[:, f, :].bitcast(F32), ALU.subtract)
                v.drain().then_inc(ckvn.sem, 1)

                dve.wait_ge(free["u"].sem, free["u"].at(l, KD))
                v.tensor_copy(pool_last[:, :, 0:CTX], uext[:, :, US - CTX:US])
                for b in range(NB):
                    o = US + b * (CTX + NS) + NS
                    v.tensor_copy(pool_last[:, :, CTX * (b + 1):CTX * (b + 2)], uext[:, :, o:o + CTX])
                v.drain().then_inc(last_ready.sem, 1)

                def window_mean(g):
                    u = uext[:, 2 * g:2 * g + 2, :]
                    src, d = u, 1
                    for n in range(g + 1):
                        dst = win if (g - n) % 2 == 0 else win2[g]
                        v.tensor_tensor(dst[:, :, 2 * d - 1:], src[:, :, 2 * d - 1:], src[:, :, d - 1:UE - d], ALU.add)
                        v.drain()
                        src, d = dst, 2 * d
                    v.tensor_tensor(win[:, :, CTX:CTX + 15], win[:, :, CTX:CTX + 15], ramp[:, g:g + 1, 0:15].broadcast_to([128, 2, 15]), ALU.mult)
                    v.drain()
                    v.scalar_tensor_tensor(win[:, :, CTX:], win[:, :, CTX:], 1.0 / WINDOWS[g], u[:, :, CTX:], ALU.mult, ALU.subtract)
                    v.drain()

                    def parts(t):
                        yield t[:, :, 0:TP], win[:, :, CTX:US], slice(0, TP)
                        for e in range(2):
                            yield (t[:, e, TP:T].rearrange("p (b c) -> p b c", b=NB),
                                   win[:, e, US:UE].rearrange("p (b c) -> p b c", b=NB)[:, :, CTX:], e)

                    for out, val, _ in parts(y_hi[g]):
                        v.tensor_copy(out, val)
                    v.drain()
                    for (out, val, _), (part, _, _) in zip(parts(y_lo[g]), parts(y_hi[g])):
                        v.tensor_tensor(out, val, part.bitcast(F32), ALU.subtract)
                    v.drain().then_inc(y_ready.sem, 1)

                window_mean(0)
                dve.wait_ge(free["uq"].sem, free["uq"].at(l, 12))
                dve.sem_inc(passed[2], 1)
                for t in range(4):
                    v.stream_shuffle(tmp[:, 0, :], qr[:, t, :], mask=half_turn)
                    v.tensor_tensor(qr[:, t, :], qr[:, t, :], rope[:, 0, :], ALU.mult)
                    v.drain()
                    v.tensor_tensor(tmp[:, 0, :], tmp[:, 0, :], rope[:, 1, :], ALU.mult)
                    v.drain()
                    v.tensor_tensor(qr[:, t, :], qr[:, t, :], tmp[:, 0, :], ALU.add)
                    v.drain()
                v.drain().then_inc(q_roped.sem, 1)
                for g in range(1, 4):
                    window_mean(g)
                for m in range(KD):
                    dve.wait_ge(full["pool"].sem, full["pool"].at(l, m + 1))
                    v.tensor_scalar(two(uext[:, m, 0:T]), bank_pair(m), par[:, P_PS + m:P_PS + m + 1], None, ALU.mult).then_inc(free["pool"].sem, 1)
                v.drain()
                with dve.Fori(0, KD // 2) as i:
                    for s in range(2):
                        dve.wait_ge(free["g"].sem, free["g"].at(l, 2 * i + (s + 1)))
                        z = flat(uext[:, bass.ds(2 * i + s, 1), 0:T])
                        v.tensor_tensor(z, z, tmp[:, s, :], ALU.mult).then_inc(gated.sem, 1)

                v.drain()
                dve.wait_ge(free["uv"].sem, free["uv"].at(l, 4))
                for s in range(2):
                    v.tensor_copy(k96[DN:96, s, :], krope[:, 0:TP])
                for j in range(4):
                    for t in range(4):
                        v.tensor_copy(qrs[:, :, 4 * t + j, :], by_seq(qr[32 * j:32 * j + 32, t, TP:T]))

                def out_head(p, s, n):
                    dve.wait_ge(pv.sem, pv.at(l, n))
                    gb = flat(gate_b[64 * s:64 * s + 64, bass.ds(p, 1), 0:TP])
                    v.tensor_tensor(gb, gb, PS[64 * s:64 * s + 64, 7, :], ALU.mult).then_inc(o_done.sem, 1)

                def prompt_head(i, j):
                    h = 4 * i + j
                    s = j % 2
                    if not isinstance(i, int) or h >= 2:
                        dve.wait_ge(pv.sem, pv.at(l, h - 1))
                    v.tensor_copy(v64[:, s], vn[:, :, bass.ds(DV * h, DV)]).then_inc(v_asm.sem, 1)
                    for qb in range(4):
                        dve.wait_ge(qk.sem, qk.at(l, 4 * h + (qb + 1)))
                        diag = PS[:, qb, 128 * qb:128 * qb + 128]
                        v.tensor_tensor(diag, diag, causal[:], ALU.add)
                        v.drain()
                        v.tensor_reduce(softm[:, qb:qb + 1], PS[:, qb, 0:128 * (qb + 1)], AX.X, ALU.max)
                        v.drain()
                        v.tensor_scalar(softm[:, 4 + qb:5 + qb], softm[:, qb:qb + 1], -SCALE, None, ALU.mult).then_inc(smax.sem, 1)
                    for qb in range(4):
                        dve.wait_ge(expd.sem, expd.at(l, 4 * h + (qb + 1)))
                        v.reciprocal(softm[:, 12 + qb:13 + qb], softm[:, 8 + qb:9 + qb])
                        v.drain()
                        o = 64 * qb * (qb + 1)
                        pr = prob[:, o:o + 128 * (qb + 1)]
                        v.tensor_scalar(pr, pr, softm[:, 12 + qb:13 + qb], None, ALU.mult)
                    v.drain().then_inc(normed.sem, 1)
                    if not isinstance(i, int) or h >= 1:
                        out_head(2 * i + (j - 1) // 2, (j - 1) % 2, h)

                for j in range(4):
                    prompt_head(0, j)
                with dve.Fori(1, 4) as i:
                    for j in range(4):
                        prompt_head(i, j)
                out_head(7, 1, 16)
                v.drain()

                dve.wait_ge(qlat_ev.sem, qlat_ev.at(l, 1))
                dve.sem_inc(passed[2], 1)
                with dve.Fori(0, NB // 2) as i:
                    for s in range(2):
                        b = 2 * i + s
                        v.tensor_copy(qst[:, s, 0:2, :].rearrange("p c (h s) -> p c h s", h=NH), qlat[:, :, bass.ds(b, 1), :, :].rearrange("p c b h s -> p c (b h) s"))
                        v.tensor_copy(qst[0:DR, s, 2, :], qrs[:, bass.ds(b, 1), :, :].rearrange("p b h s -> p (b h s)")).then_inc(qst_ready.sem, 1)

                        def keys(g):
                            dve.wait_ge(kt_p.sem, kt_p.at(l, 4 * b + (g + 1)))
                            v.tensor_copy(keysT[g % 2][:, 0, :], PS[:, 0, :])
                            v.tensor_copy(keysT[g % 2][0:DR, 2, :], PS[0:DR, 2, :]).then_inc(kt_d.sem, 1)

                        def scores(g):
                            dve.wait_ge(s_p.sem, s_p.at(l, 5 * b + (g + 1)))
                            w = 512 if g < 4 else NS
                            if g == 4:
                                v.tensor_tensor(PS[:, 3, 0:w], PS[:, 3, 0:w], causal_s[:], ALU.add)
                                v.drain()
                            v.tensor_reduce(softm[:, 16 + g:17 + g], PS[:, 3 + g % 2, 0:w], AX.X, ALU.max).then_inc(s_d.sem, 1)

                        keys(0)
                        for g in range(4):
                            if g < 3:
                                keys(g + 1)
                            scores(g)
                        scores(4)
                        v.drain()
                        v.tensor_reduce(softm[:, 21:22], softm[:, 16:21], AX.X, ALU.max)
                        v.drain()
                        v.tensor_scalar(softm[:, 24:25], softm[:, 21:22], -SCALE, None, ALU.mult).then_inc(s_max.sem, 1)
                        dve.wait_ge(s_exp.sem, s_exp.at(l, b + 1))
                        v.reciprocal(softm[:, 26:27], softm[:, 25:26])
                        for g in (1, 3):
                            dve.wait_ge(spt_p.sem, spt_p.at(l, 5 * b + (g + 1)))
                            v.tensor_copy(pT[:, 4 * g:4 * g + 4, :].rearrange("p a b -> p (a b)"), PS[:, 6, :]).then_inc(spt_d.sem, 1)
                        dve.wait_ge(spt_p.sem, spt_p.at(l, 5 * b + 5))
                        v.tensor_copy(pT[0:NS, NPG, :], PS[0:NS, 5, 0:128]).then_inc(spt_d.sem, 1)
                        dve.wait_ge(spv.sem, spv.at(l, b + 1))
                        v.tensor_scalar(olat[:], PS[:, 7, 0:KVL], softm[:, 26:27], None, ALU.mult).then_inc(so_d.sem, 1)
                dve.wait_ge(uvs.sem, uvs.at(l, 1))
                v.tensor_tensor(gate_b[:, :, TP:T], gate_b[:, :, TP:T], PS[:, 0, :].rearrange("p (a b) -> p a b", a=KD), ALU.mult)
                v.drain()

                for f in range(KD):
                    s = f % 2
                    v.tensor_tensor(tmp[:, s, :], gate_b[:, f, :], uext[:, f, 0:T], ALU.add)
                    v.drain()
                    v.tensor_copy(h_hi[:, f, :], tmp[:, s, :])
                    v.drain()
                    v.tensor_tensor(h_lo[:, f, :], tmp[:, s, :], h_hi[:, f, :].bitcast(F32), ALU.subtract)
                v.drain().then_inc(mixed.sem, 1)
                residual(l, "out", 16, U_OUT, 1)
                v.drain().then_inc(x_mid.sem, 1)

                norm(l, 1, 3, gain2, 24)
                v.memset(zext[:, :, 0:2], 0.0)
                v.drain().then_inc(h_ready.sem, 1)
                with dve.Fori(0, KF) as j:
                    for s in range(2):
                        f = j + KF * s
                        c = conv[:, s, 0:ZE - 2]
                        dve.wait_ge(t0.sem, t0.at(l, 2 * j + (s + 1)))
                        v.scalar_tensor_tensor(c, zext[:, s, 1:ZE - 1], convp[:, 0, bass.ds(f + 2 * KF, 1)], c, ALU.mult, ALU.add)
                        v.drain()
                        v.scalar_tensor_tensor(c, zext[:, s, 0:ZE - 2], convp[:, 0, bass.ds(f, 1)], c, ALU.mult, ALU.add).then_inc(zconv.sem, 1)
                    v.drain()
                    dve.wait_ge(silud.sem, silud.at(l, j + 1))
                    v.tensor_tensor(conv[:, 0, 0:ZE - 2], conv[:, 0, 0:ZE - 2], conv[:, 1, 0:ZE - 2], ALU.mult).then_inc(prod.sem, 1)
                    v.drain()
                    dve.wait_ge(act_hi_done.sem, act_hi_done.at(l, j + 1))
                    ah, al = flat(act_hi[:, bass.ds(j, 1), :]).bitcast(F32), flat(act_lo[:, bass.ds(j, 1), :])
                    v.tensor_tensor(al[:, 0:TP], conv[:, 0, 0:TP], ah[:, 0:TP], ALU.subtract)
                    v.tensor_tensor(by_seq(al[:, TP:T]), by_seq(conv[:, 0, ZS:ZE])[:, :, 0:NS], by_seq(ah[:, TP:T]), ALU.subtract).then_inc(act_ready.sem, 1)
                v.drain()
                residual(l, "down", 40, U_DOWN, 3)
                v.drain().then_inc(x_new.sem, 1)

            sum_squares(DEPTH, 0, D)
            dve.wait_ge(root.sem, root.at(DEPTH, 1))
            v.reciprocal(rinv[:], rinv[:])
            v.drain()
            for f in range(KD):
                v.scalar_tensor_tensor(yT[:, f, :], x[:, f, :], g_fin[:, f:f + 1], rinv[:], ALU.mult, ALU.mult)
            v.drain().then_inc(fin_norm.sem, 1)

        @block.tensor
        def _(pe):
            mm = nc.tensor.matmul
            pe.sem_inc(unit_used.sem, 2)
            pe.sem_inc(spv.sem, 2)
            pe.sem_inc(ada_T.sem, 2)

            def turn(out, src, k):
                return nc.tensor.transpose(out, src, ident[0:k, 0:k])

            pe.wait_ge(x_in.sem, 32)
            pe.wait_ge(const_in.sem, 16 * 9)
            for f in range(KD):
                if f >= 2:
                    pe.wait_ge(start_ev.sem, f - 1)
                for n in range(4):
                    turn(PS[:, 2 * (f % 2), 128 * n:128 * n + 128], rows_in[:, n, 128 * f:128 * f + 128], 128)
                turn(PS[:, 2 * (f % 2) + 1, 0:TS], rows_in[0:TS, 4, 128 * f:128 * f + 128], TS).then_inc(start_T.sem, 1)
            for f in range(KD):
                turn(PS[:, 4, NC * f:NC * f + NC], c_rows[:, 128 * f:128 * f + 128], NC)
            turn(PS[:, 4, 128:128 + KD], gf_rows[:], KD).then_inc(start_T.sem, 1)
            pe.wait_ge(start_ev.sem, KD)
            pe.wait_ge(cond_ready.sem, 1)

            def use(l, u):
                pe.wait_ge(lo_ready.sem, lo_ready.at(l, u + 1))

            def weights(part, slot, k, m):
                return part[:, slot, m * k:m * k + m]

            def products(slot, nk, xh, xl, k0, j, first=True, last=True, m=128):
                for k in range(nk):
                    for part, operands in ((whi, (xh, xl)), (wlo, (xh,))):
                        w = weights(part, slot, k, m)
                        for o in operands:
                            for half in range(2):
                                r = mm(PS[0:m, 2 * (j % 2) + half, 0:HT], w, o[:, k0 + k, half * HT:half * HT + HT],
                                       start=(first and k == 0 and part is whi and o is xh), stop=(last and k == nk - 1 and part is wlo))
                return r

            def dense(l, phase, u0, n, nk, xh, xl, base=0):
                with pe.Fori(0, n // 2) as i:
                    for s in range(2):
                        use(l, 2 * i + (u0 + s))
                        pe.wait_ge(free[phase].sem, free[phase].at(l, 2 * i + (base + s - 1)))
                        products(s, nk, xh, xl, 0, s).then_inc(unit_used.sem, 1)

            def banks_free_of(l, phase):
                pe.wait_ge(free[phase].sem, free[phase].at(l, N_TILE[phase]))
                pe.sem_inc(passed[3], 1)

            def over_partitions(l, src, k):
                pe.wait_ge(ssum.sem, ssum.at(l, k + 1))
                for half in range(2):
                    r = mm(PS[:, 6 + half, 0:HT], ones[:], src[:, half * HT:half * HT + HT], start=True, stop=True)
                r.then_inc(ssum_p.sem, 1)

            with pe.Fori(0, DEPTH) as l:
                pe.wait_ge(x_new.sem, x_new.at(l, 0))
                pe.wait_ge(cl_ev.sem, cl_ev.at(l, 0))
                pe.wait_ge(par_in.sem, par_in.at(l, 16 * PAR_LOADS))
                turn(PS[:, 4, 0:80], rows[0:80, 0, :], 80)
                turn(PS[:, 4, 80:168], rows[0:88, 1, :], 88)
                turn(PS[:, 4, 168:256], rows[0:88, 2, :], 88)
                for c in range(4):
                    turn(PS[:, 5, 128 * c:128 * c + 128], rows[:, 3 + c, :], 128)
                turn(PS[:, 4, 256:384], rows[:, 7, :], 128)
                turn(PS[:, 4, 384:448], rows[0:64, 8, :], 64)
                for c in range(7):
                    turn(PS[:, 6 + c // 4, 128 * (c % 4):128 * (c % 4) + 128], rows[:, 9 + c, :], 128)
                turn(PS[:, 7, 384:448], rows[0:64, 16, :], 64).then_inc(par_T.sem, 1)
                pe.wait_ge(par_ev.sem, par_ev.at(l, 1))
                pe.sem_inc(passed[3], 1)

                with pe.Fori(0, 24) as i:
                    for s in range(2):
                        use(l, 2 * i + s)
                        for k in range(KD):
                            for part in (whi, wlo):
                                r = mm(PS[0:2 * NC, 4 + s, 0:128], cond[:, k, :], part[:, s, 128 * k:128 * k + 128],
                                       start=(k == 0 and part is whi), stop=(k == KD - 1 and part is wlo))
                        r.then_inc(unit_used.sem, 1)
                        pe.wait_ge(ada_ev.sem, ada_ev.at(l, 2 * i + (s + 1)))
                        mm(PS[:, 6, bass.ds(NC * (2 * i + s), NC)], ada_rows[:, s, :], fold[:], start=True, stop=True).then_inc(ada_T.sem, 1)
                over_partitions(l, sumsq, 0)

                pe.wait_ge(h_ready.sem, h_ready.at(l, 1))
                pe.sem_inc(passed[3], 1)
                dense(l, "qkv", U_CQ, 8, KD, h_hi, h_lo)
                pe.wait_ge(free["qkv"].sem, free["qkv"].at(l, 7))
                for s in range(2):
                    use(l, U_KR + s)
                    products(s, 4, h_hi, h_lo, 4 * s, 0, first=s == 0, last=s == 1, m=DR).then_inc(unit_used.sem, 1)
                banks_free_of(l, "qkv")
                dense(l, "u", U_U, 4, KD, h_hi, h_lo)
                over_partitions(l, sumsq, 1)
                pe.wait_ge(root.sem, root.at(l, 2))
                over_partitions(l, kv_sum[:, 0, :], 2)
                dense(l, "u", U_U + 4, 4, KD, h_hi, h_lo, 4)

                pe.wait_ge(root.sem, root.at(l, 3))
                pe.wait_ge(last_ready.sem, last_ready.at(l, 1))
                for f in range(KD):
                    o = 128 * (f % 4)
                    turn(PS[0:NB * CTX, 4 + f // 4, o:o + 128], pool_last[:, f, CTX:], 128)
                    r = turn(PS[0:CTX, 6 + f // 4, o:o + 128], pool_last[:, f, 0:CTX], 128)
                r.then_inc(last_T.sem, 1)
                pe.wait_ge(last_ev.sem, last_ev.at(l, 1))
                pe.wait_ge(ckvn.sem, ckvn.at(l, 1))
                for n in range(5):
                    m = 128 if n < 4 else TS
                    if n >= 2:
                        pe.wait_ge(lat_ev.sem, lat_ev.at(l, n - 1))
                        pe.sem_inc(passed[3], 1)
                    for c in range(KC):
                        turn(PS[0:m, 4 + n % 2, 128 * c:128 * c + 128], ckv[:, c, 128 * n:128 * n + m], 128)
                    turn(PS[0:m, 4 + n % 2, KVL:LAT], krope[:, 128 * n:128 * n + m], DR).then_inc(lat_T.sem, 1)

                pe.wait_ge(cqn.sem, cqn.at(l, 1))
                banks_free_of(l, "u")
                dense(l, "uq", U_QN, 8, KQ, cq_hi, cq_lo)
                dense(l, "uq", U_QR, 4, KQ, cq_hi, cq_lo, 8)

                def few_pieces(s, w0, step, xh, xl, out):
                    for k in range(2):
                        for part, operands in ((whi, (xh, xl)), (wlo, (xh,))):
                            for o in operands:
                                for bank, (c0, c1) in out:
                                    r = mm(PS[:, bank, 0:c1 - c0], part[:, s, w0 + step * k:w0 + step * k + 128], o[:, k, c0:c1],
                                           start=(k == 0 and part is whi and o is xh), stop=(k == 1 and part is wlo))
                    return r

                banks_free_of(l, "uq")
                for s in range(2):
                    use(l, U_POOL + s)
                    for g in (2 * s, 2 * s + 1):
                        pe.wait_ge(y_ready.sem, y_ready.at(l, g + 1))
                        for m in (2 * g, 2 * g + 1):
                            pe.wait_ge(free["pool"].sem, free["pool"].at(l, m - 1))
                            b = 2 * (m % 2)
                            few_pieces(s, 512 * (g % 2) + 128 * (m % 2), 256, y_hi[g], y_lo[g],
                                       ((b, (0, HT)), (b + 1, (HT, T)))).then_inc(full["pool"].sem, 1)
                    nc.tensor.drain().then_inc(unit_used.sem, 1)

                banks_free_of(l, "pool")
                dense(l, "g", U_G, 16, KD, h_hi, h_lo)

                banks_free_of(l, "g")
                for p in range(8):
                    s = p // 4
                    if p % 4 == 0:
                        use(l, U_UK + s)
                    pe.wait_ge(free["uk"].sem, free["uk"].at(l, p - 1))
                    b = 2 * (p % 2)
                    few_pieces(s, 128 * (p % 4), 512, ckv_hi, ckv_lo, ((b, (0, TP)),))
                    for k in range(2):
                        for part in (whi, wlo):
                            o = 512 * k + 128 * (p % 4)
                            r = mm(PS[:, b + 1, 128 * k:128 * k + 128], part[:, s, o:o + 128], ident_r[:], start=part is whi, stop=part is wlo)
                    r.then_inc(full["uk"].sem, 1)
                    if p % 4 == 3:
                        nc.tensor.drain().then_inc(unit_used.sem, 1)
                banks_free_of(l, "uk")
                for n in range(4):
                    s = n // 2
                    if n % 2 == 0:
                        use(l, U_UV + s)
                    pe.wait_ge(free["uv"].sem, free["uv"].at(l, n - 1))
                    for kb in (2 * (n % 2), 2 * (n % 2) + 1):
                        for k in range(2):
                            for o, parts in ((ckv_hi, (whi, wlo)), (ckv_lo, (whi,))):
                                for part in parts:
                                    r = mm(PS[:, kb, :], o[:, k, 128 * kb:128 * kb + 128], part[:, s, 512 * k:512 * k + 512],
                                           start=(k == 0 and o is ckv_hi and part is whi), stop=(k == 1 and o is ckv_lo))
                    r.then_inc(full["uv"].sem, 1)
                    if n % 2 == 1:
                        nc.tensor.drain().then_inc(unit_used.sem, 1)
                pe.wait_ge(lat_ev.sem, lat_ev.at(l, 5))
                for h in range(NH):
                    p, s = h // 2, 64 * (h % 2)
                    for c in range(KC):
                        r = mm(PS[:, 4 + 2 * c + h % 2, 64 * p:64 * p + 64], wukT[s:s + 64, p, 128 * c:128 * c + 128],
                               qn[s:s + 64, p, TP:T], start=True, stop=True)
                r.then_inc(qlat_p.sem, 1)

                def head_scores(h, s, first=False):
                    pe.wait_ge(q_asm.sem, q_asm.at(l, h + 1))
                    pe.wait_ge(k_asm.sem, k_asm.at(l, h + 1))
                    if first:
                        pe.wait_ge(v_asm.sem, v_asm.at(l, 1))
                        banks_free_of(l, "uv")
                    for qb in range(4):
                        if not first:
                            pe.wait_ge(expd.sem, expd.at(l, 4 * h + (qb - 3)))
                        mm(PS[:, qb, 0:128 * (qb + 1)], q96[:, s, 128 * qb:128 * qb + 128], k96[:, s, 0:128 * (qb + 1)],
                           start=True, stop=True).then_inc(qk.sem, 1)

                def head_values(h, s):
                    pe.wait_ge(normed.sem, normed.at(l, h + 1))
                    pe.wait_ge(pt_ev.sem, pt_ev.at(l, h))
                    pe.wait_ge(qlat_ev.sem, qlat_ev.at(l, 1))
                    for kb in range(4):
                        for qb in range(kb, 4):
                            o = 64 * qb * (qb + 1) + 128 * kb
                            c = 128 * (qb - kb) + (256 if kb == 3 else 0)
                            r = turn(PS[:, 4 + min(kb, 2), c:c + 128], prob[:, o:o + 128], 128)
                    r.then_inc(pt_p.sem, 1)
                    pe.wait_ge(pt_ev.sem, pt_ev.at(l, h + 1))
                    pe.wait_ge(v_asm.sem, v_asm.at(l, h + 1))
                    pe.wait_ge(o_done.sem, o_done.at(l, h))
                    for kb, o in enumerate((0, 512, 896, 1152)):
                        r = mm(PS[64 * s:64 * s + 64, 7, 128 * kb:TP], v64[:, s, kb, :], probT[:, o:o + TP - 128 * kb],
                               start=kb == 0, stop=kb == 3)
                    r.then_inc(pv.sem, 1)

                head_scores(0, 0, True)
                with pe.Fori(0, 3) as i:
                    for j in range(4):
                        head_scores(4 * i + (j + 1), (j + 1) % 2)
                        head_values(4 * i + j, j % 2)
                for h in range(12, 16):
                    if h < 15:
                        head_scores(h + 1, (h + 1) % 2)
                    head_values(h, h % 2)
                pe.wait_ge(o_done.sem, o_done.at(l, NH))
                pe.sem_inc(passed[3], 1)

                with pe.Fori(0, NB // 2) as i:
                    for s in range(2):
                        b = 2 * i + s
                        pe.wait_ge(kv_in[s].sem, kv_in[s].at(l, 16 * (NPG + 1) * (i + 1)))

                        def turn_keys(g):
                            pe.wait_ge(kt_d.sem, kt_d.at(l, 4 * b + g))
                            pe.wait_ge(kt_a.sem, kt_a.at(l, 4 * b + g))
                            for j in range(4):
                                for c in range(KC):
                                    turn(PS[:, c, 128 * j:128 * j + 128], pages[s][:, 4 * g + j, 128 * c:128 * c + 128], 128)
                                r = turn(PS[0:DR, 2, 128 * j:128 * j + 128], pages[s][:, 4 * g + j, KVL:LAT], 128)
                            r.then_inc(kt_p.sem, 1)

                        def scores(g):
                            if g < 4:
                                pe.wait_ge(kt_d.sem, kt_d.at(l, 4 * b + (g + 1)))
                                pe.wait_ge(kt_a.sem, kt_a.at(l, 4 * b + (g + 1)))
                            pe.wait_ge(s_a.sem, s_a.at(l, 5 * b + (g - 1 if g >= 2 else 0)))
                            for c in range(3):
                                k = 128 if c < 2 else DR
                                if g < 4:
                                    keys, w = keysT[g % 2][0:k, c, :], 512
                                else:
                                    keys, w = (ckv[:, c, bass.ds(TP + NS * b, NS)] if c < 2 else krope[:, bass.ds(TP + NS * b, NS)]), NS
                                r = mm(PS[:, 3 + g % 2, 0:w], qst[0:k, s, c, :], keys, start=c == 0, stop=c == 2)
                            r.then_inc(s_p.sem, 1)

                        turn_keys(0)
                        pe.wait_ge(qst_ready.sem, qst_ready.at(l, b + 1))
                        for g in range(4):
                            if g < 3:
                                turn_keys(g + 1)
                            scores(g)
                        scores(4)
                        pe.wait_ge(s_exp.sem, s_exp.at(l, b + 1))
                        for g in range(5):
                            e, k = ((spt_d, 3 * b), (spt_d, 3 * b), (spt_a, 2 * b + 1), (spt_d, 3 * b + 1), (spt_a, 2 * b + 2))[g]
                            pe.wait_ge(e.sem, e.at(l, k))
                            if g < 4:
                                for j in range(4):
                                    o = 512 * g + 128 * j
                                    r = turn(PS[:, 5 + g % 2, 128 * j:128 * j + 128], sc[:, o:o + 128], 128)
                            else:
                                r = turn(PS[0:NS, 5, 0:128], sc[:, PAST:PAST + NS], 128)
                            r.then_inc(spt_p.sem, 1)
                        pe.wait_ge(spt_a.sem, spt_a.at(l, 2 * b + 2))
                        pe.wait_ge(spt_d.sem, spt_d.at(l, 3 * b + 3))
                        pe.wait_ge(so_a.sem, so_a.at(l, b))
                        for j in range(NPG):
                            mm(PS[:, 7, 0:KVL], pT[:, j, :], pages[s][:, j, 0:KVL], start=j == 0, stop=False)
                        mm(PS[:, 7, 0:KVL], pT[0:NS, NPG, :], newk[:, s, 0:KVL], start=False, stop=True).then_inc(spv.sem, 1)
                        pe.wait_ge(so_d.sem, so_d.at(l, b + 1))
                        for c in range(KC):
                            r = turn(PS[:, 7, 256 + 128 * c:384 + 128 * c], olat[:, 128 * c:128 * c + 128], 128)
                        r.then_inc(so_T.sem, 1)
                pe.wait_ge(so_a.sem, so_a.at(l, NB))
                pe.wait_ge(wuv_in.sem, wuv_in.at(l, 16))
                for h in range(NH):
                    p, s = h // 2, 64 * (h % 2)
                    for c in range(KC):
                        r = mm(PS[s:s + 64, 0, 64 * p:64 * p + 64], wuv[:, c, DV * h:DV * h + DV], olatT[:, c, h].rearrange("p b s -> p (b s)"),
                               start=c == 0, stop=c == KC - 1)
                r.then_inc(uvs.sem, 1)

                pe.wait_ge(mixed.sem, mixed.at(l, 1))
                pe.sem_inc(passed[3], 1)
                dense(l, "out", U_OUT, 8, KD, h_hi, h_lo)
                over_partitions(l, sumsq, 3)
                pe.wait_ge(h_ready.sem, h_ready.at(l, 2))
                pe.sem_inc(passed[3], 1)
                dense(l, "up", U_UP, 44, KD, h_hi, h_lo)
                pe.wait_ge(act_ready.sem, act_ready.at(l, KF))
                for n in range(11):
                    if n >= 2:
                        pe.wait_ge(cl_ev.sem, cl_ev.at(l, n - 1))
                    for f in range(4 * n, 4 * n + 4):
                        r = turn(PS[0:2 * NC, 4 + n % 2, 128 * (f % 4):128 * (f % 4) + 128], conv_last[:, f, :], 128)
                    r.then_inc(cl_T.sem, 1)
                banks_free_of(l, "up")
                with pe.Fori(0, 4) as i:
                    for t in range(2):
                        pe.wait_ge(free["down"].sem, free["down"].at(l, 2 * i + (t - 1)))
                        for c in range(3):
                            w = 3 * t + c
                            use(l, 6 * i + (U_DOWN + w))
                            products(w % 2, min(8, KF - 8 * c), act_hi, act_lo, 8 * c, t, first=c == 0, last=c == 2).then_inc(unit_used.sem, 1)

            pe.wait_ge(x_new.sem, x_new.at(DEPTH, 0))
            over_partitions(DEPTH, sumsq, 0)
            pe.wait_ge(fin_norm.sem, 1)
            for n in range(5):
                m = 128 if n < 4 else TS
                if n >= 2:
                    pe.wait_ge(fin_ev.sem, n - 1)
                for f in range(KD):
                    o = 128 * (f % 4)
                    r = turn(PS[0:m, 2 * (n % 2) + f // 4, o:o + 128], yT[:, f, 128 * n:128 * n + m], 128)
                r.then_inc(fin_T.sem, 1)


_ORDER = ["x_prompt", "x_sample", "cache_latent", "state_pool", "state_conv", "page_table", "c_prompt", "c_sample",
          "w_ada", "b_ada", "g_attn", "w_in", "g_q", "w_uq", "g_kv", "w_uk", "w_uv", "w_pool", "pool_scale", "w_out",
          "g_ffn", "w_up", "w_conv", "b_conv", "w_down", "g_final"]
_OUT = [("y_p", (1, TP, D)), ("y_s", (NB, NS, D)), ("lat_p", (DEPTH, 1, TP, LAT)), ("pool_p", (DEPTH, 1, CTX, D)),
        ("conv_p", (DEPTH, 1, 2, 2 * DF)), ("lat_s", (DEPTH, NB, NS, LAT)), ("pool_s", (DEPTH, NB, CTX, D)),
        ("conv_s", (DEPTH, NB, 2, 2 * DF))]


def constants():
    tok = np.arange(128)
    half = DR // 2
    freq = np.float32(10000.0) ** (-np.arange(half, dtype=np.float32) / np.float32(half))
    pos = np.concatenate([np.arange(TP), np.tile(PAST + np.arange(NS), NB)]).astype(np.float32)
    ang = (pos[None, :] * freq[:, None]).astype(np.float32)
    cos, sin = np.cos(ang), np.sin(ang)
    rope = np.stack([np.tile(np.concatenate([cos, cos]), (4, 1)), np.tile(np.concatenate([-sin, sin]), (4, 1))], 1)
    ramp = np.ones((4, 16), np.float32)
    for g, w in enumerate(WINDOWS):
        ramp[g, :15] = w / np.minimum(np.arange(15) + 1.0, w)
    return {
        "ident": np.eye(128, dtype=np.float32),
        "ones": np.ones((128, 128), np.float32),
        "causal": np.where(tok[None, :] <= tok[:, None], 0, -1e30).astype(np.float32),
        "causal_s": np.where(np.arange(NS)[None, :] <= (tok % NS)[:, None], 0, -1e30).astype(np.float32),
        "fold": np.tile(np.eye(NC, dtype=np.float32), (2, 1)),
        "ramp": np.tile(ramp.reshape(1, 64), (128, 1)).astype(np.float32),
        "rope": np.ascontiguousarray(rope.reshape(128, 2 * T)).astype(np.float32),
    }


def kernel(**inputs):
    import concourse.bacc as bacc
    from concourse.bass_utils import run_bass_kernel_spmd

    nc = bacc.Bacc("TRN2", target_bir_lowering=False, num_devices=1)
    arrays, A, O = {}, {}, {}
    for name in _ORDER:
        arrays[name] = np.ascontiguousarray(inputs[name])
    for name, a in constants().items():
        arrays["t_" + name] = a
    for name, a in arrays.items():
        A[name.removeprefix("t_")] = nc.dram_tensor(name, a.shape, mybir.dt.from_np(a.dtype), kind="ExternalInput").ap()
    for name, shape in _OUT:
        O[name] = nc.dram_tensor("o_" + name, shape, F32, kind="ExternalOutput").ap()
    build(nc, A, O)
    r = run_bass_kernel_spmd(nc, [arrays], core_ids=[0]).results[0]
    return tuple(r["o_" + name] for name, _ in _OUT)
```

```python
import numpy as np
import concourse.bass as bass
from concourse import mybir

F32 = mybir.dt.float32
F32R = mybir.dt.float32r
I32 = mybir.dt.int32
ALU = mybir.AluOpType
ACT = mybir.ActivationFunctionType
AX = mybir.AxisListType

D = 1024
DEPTH = 2
TP, NB, NS = 512, 8, 8
TS = NB * NS
T = TP + TS
HT = T // 2
PAST, PAGE = 2048, 128
NPG = PAST // PAGE
NH, DN, DR, DV = 16, 64, 32, 64
KVL, QL = 256, 768
LAT = KVL + DR
SCALE = float((DN + DR) ** -0.5)
WINDOWS = (2, 4, 8, 16)
CTX = 15
DF = 2816
EPS = 1e-6
KD, KQ, KF = D // 128, QL // 128, DF // 128
KC = KVL // 128
UE = CTX + TP + NB * (CTX + NS)
US = CTX + TP
ZE = 2 + TP + NB * (2 + NS)
ZS = 2 + TP
NC = 1 + NB

U_CQ, U_KV, U_KR, U_U = 0, 6, 8, 10
U_QN, U_QR, U_POOL, U_GB, U_UK, U_UV, U_OUT, U_UP, U_DOWN, UNITS = 18, 26, 30, 42, 50, 52, 54, 62, 106, 130
ADA = 6 * KD

C_KV, C_KR, C_U, C_G = QL, QL + KVL, QL + KVL + DR, QL + KVL + DR + D

P_GA, P_GF, P_PS, P_BA, P_GQ, P_GK, P_ALL = 0, 8, 16, 24, 72, 78, 80


class Signal:

    def __init__(self, sem, per_layer, ahead=0):
        self.sem, self.per_layer, self.ahead = sem, per_layer, ahead

    def at(self, l, k):
        return l * self.per_layer + (k + self.ahead)


def build(nc, A, O):
    base = 16512
    place = [base]

    def keep(name, shape, dt=F32):
        size = int(np.prod(shape[1:])) * 4
        t = nc.alloc_sbuf_tensor_at(name, shape, dt, offset=place[0])
        place[0] += (size + 31) // 32 * 32
        return t

    x = keep("x", [128, KD, T])
    raw = keep("raw", [128, 2, 1024])
    whi = keep("whi", [128, 2, 1024], F32R)
    wlo = keep("wlo", [128, 2, 1024], F32R)
    ident = keep("ident", [128, 128])
    ident_r = keep("ident_r", [128, 128], F32R)
    ones = keep("ones", [128, 128])
    causal = keep("causal", [128, 128])
    causal_s = keep("causal_s", [128, NS])
    ramp = keep("ramp", [128, 4, 16])
    par = keep("par", [128, P_ALL])
    convp = keep("convp", [128, 2, 2 * 2 * KF])
    conv_prev = keep("conv_prev", [128, 2 * NB, 2 * KF])
    mod = keep("mod", [128, 6 * KD, NC])
    gain1 = keep("gain1", [128, KD, NC])
    gain2 = keep("gain2", [128, KD, NC])
    cond = keep("cond", [128, KD, NC])
    g_fin = keep("g_fin", [128, KD])
    eps = keep("eps", [128, 1])
    softm = keep("softm", [128, 32])
    tab = keep("tab", [1, NB * NPG], I32)
    work = place[0]
    sumsq = keep("sumsq", [128, T])
    rinv = keep("rinv", [128, T])
    tmp = keep("tmp", [128, 2, T])
    arena = place[0]

    def at(name, shape, off, dt=F32):
        return nc.alloc_sbuf_tensor_at(name, shape, dt, offset=off)

    ada_w = at("ada_w", [128, 6, 1024], base + (KD * T * 4 + 31) // 32 * 32)
    B = T * 4
    h_hi = at("h_hi", [128, KD, T], arena, F32R)
    h_lo = at("h_lo", [128, KD, T], arena + KD * B, F32R)
    a = arena + 2 * KD * B
    uext = at("uext", [128, KD, UE], a)
    a += KD * UE * 4
    cq_at = a
    cq_hi = at("cq_hi", [128, KQ, T], a, F32R)
    cq = at("cq", [128, KQ, T], a + KQ * B)
    cq_lo = at("cq_lo", [128, KQ, T], a + KQ * B, F32R)
    a += 2 * KQ * B
    y0_at = a
    a += 4 * B
    ckv_at = a
    ckv_hi = at("ckv_hi", [128, KC, T], a, F32R)
    ckv_lo = at("ckv_lo", [128, KC, T], a + KC * B, F32R)
    a += 2 * KC * B
    ckv = at("ckv", [128, KC, T], a)
    a += KC * B
    krope = at("krope", [DR, T], a)
    a += B
    q_at = a
    qn = at("qn", [128, KD, T], a)
    qr = at("qr", [128, 4, T], a + KD * B)
    a += 12 * B
    end_at = a
    rope = at("rope", [128, 2, T], a)
    a += 2 * B
    gate_a = at("gate_a", [128, 2, T], a)
    assert a + 2 * B <= 229376, a
    y_hi = [at(f"y_hi{g}", [128, 2, T], o, F32R) for g, o in enumerate((y0_at, cq_at, cq_at + 4 * B, cq_at + 8 * B))]
    y_lo = [at(f"y_lo{g}", [128, 2, T], o + 2 * B, F32R)
            for g, o in enumerate((y0_at, cq_at, cq_at + 4 * B, cq_at + 8 * B))]
    win = at("win", [128, 2, UE], work)
    win2 = [None] + [at(f"win2_{g}", [128, 2, UE], o) for g, o in enumerate((cq_at, cq_at + 4 * B, cq_at + 8 * B), 1)]
    kv_sum = at("kv_sum", [128, 2, T], q_at + 9 * B)
    rows = at("rows", [128, 17, 128], q_at)
    pool_prev = at("pool_prev", [128, NB * CTX, KD], q_at + 17 * 512)
    pool_last = at("pool_last", [128, KD, CTX + NB * CTX], q_at)
    pool_rows = at("pool_rows", [128, 2, 2, 512], q_at + 8 * 135 * 4 + 64)
    lat_rows = at("lat_rows", [128, 5, LAT], q_at + 12608)
    gate_b = at("gate_b", [128, KD, T], cq_at)
    kn = at("kn", [128, KD, TP], arena)
    wukT = at("wukT", [128, KD, KVL], arena + 16384)
    qlat = at("qlat", [128, KC, NB, NH, NS], arena + 24576)
    qrs = at("qrs", [DR, NB, NH, NS], arena + 32768)
    vn = at("vn", [128, 4, NH * DV], cq_at + KD * B)
    q96 = at("q96", [96, 2, TP], ckv_at)
    k96 = at("k96", [96, 2, TP], ckv_at + 4096)
    NP = 1280
    prob = at("prob", [128, NP], work)
    v64 = at("v64", [128, 2, 4, DV], work + NP * 4)
    probT = at("probT", [128, NP], end_at)
    pages = [at("pages0", [128, NPG, LAT], arena), at("pages1", [128, NPG, LAT], cq_at + KD * B)]
    keysT = [at("keysT0", [128, 3, 512], arena + 18432), at("keysT1", [128, 3, 512], ckv_at)]
    KS = PAST + NS
    sc = at("sc", [128, KS], end_at)
    pT = at("pT", [128, NPG + 1, 128], work)
    wuv = at("wuv", [128, KC, NH * DV], q_at)
    olatT = at("olatT", [128, KC, NH, NB, NS], q_at + 8192)
    olat = at("olat", [128, KVL], q_at + 16384)
    newk = at("newk", [NS, 2, LAT], q_at + 16384 + 1024)
    qst = at("qst", [128, 2, 3, 128], q_at + 16384 + 1024 + 2304)
    assert 16384 + 1024 + 2304 + 3072 <= 12 * B
    ada_rows = at("ada_rows", [NC, 3, 256], arena + 24576)
    a = arena + 2 * KD * B
    act_hi = at("act_hi", [128, KF, T], a, F32R)
    act_lo = at("act_lo", [128, KF, T], a + KF * B, F32R)
    a += 2 * KF * B
    ZB = (ZE * 4 + 31) // 32 * 32
    conv = [[at("conv00", [128, ZE], a), at("conv01", [128, ZE], a + ZB)], [at("conv10", [128, ZE], work + 2 * ZB), None]]
    a += 2 * ZB
    conv_last = at("conv_last", [128, 2 * KF, 2 * NC], a)
    a += 2 * KF * 2 * NC * 4
    conv[1][1] = at("conv11", [128, ZE], a)
    assert a + ZE * 4 <= 229376, a
    zext = at("zext", [128, 2, ZE], work)
    conv_rows = at("conv_rows", [2 * NC, 2 * DF], arena)
    rows_in = at("rows_in", [128, 5, D], arena)
    c_rows = at("c_rows", [NC, D], arena + 20480)
    gf_rows = at("gf_rows", [KD, 128], arena + 28672)
    yT = at("yT", [128, KD, T], arena)
    y_rows = at("y_rows", [128, 2, D], arena + KD * B)

    PS = nc.alloc_psum_tensor("PS", [128, 8, 512], F32)

    def signal(name, per_layer=0, ahead=0):
        return Signal(nc.alloc_semaphore(name), per_layer, ahead)

    def loads_before(u):
        return sum(2 if U_QN <= w < U_QR else 4 if U_QR <= w < U_POOL else 1 for w in range(u % 2, u, 2))

    LOADS = loads_before(UNITS)
    assert LOADS == loads_before(UNITS + 1)
    loaded = [signal("loaded0"), signal("loaded1")]
    hi_ready = signal("hi_ready", UNITS)
    lo_ready = signal("lo_ready", UNITS, 2)
    unit_used = signal("unit_used", UNITS, 2)

    N_TILE = dict(qkv=10, u=8, uq=12, pool=8, g=16, uk=8, uv=4, out=8, up=44, down=8)
    full = {k: signal(f"full_{k}", N_TILE[k]) for k in ("pool", "uk", "uv")}
    free = {k: signal(f"free_{k}", n, 2) for k, n in N_TILE.items()}
    const_in, x_in, tab_in = signal("const_in"), signal("x_in"), signal("tab_in")
    eps_set, start_T, start_ev = signal("eps_set"), signal("start_T"), signal("start_ev")
    cond_ready = signal("cond_ready")
    fin_norm, fin_T, fin_ev = signal("fin_norm"), signal("fin_T"), signal("fin_ev")
    y_out = [signal("y_out0"), signal("y_out1")]
    PAR_LOADS = 13
    par_in, rope_in = signal("par_in", 16 * PAR_LOADS), signal("rope_in", 16)
    par_T, par_ev = signal("par_T", 1), signal("par_ev", 1)
    ada_in = [signal(f"ada_in{s}", 16 * ADA // 6) for s in range(6)]
    ada_used, ada_p = signal("ada_used", ADA, 6), signal("ada_p", ADA // 2)
    ada_ev, ada_T = signal("ada_ev", ADA // 2, 3), signal("ada_T", ADA // 2, 3)
    sq, sq_used = signal("sq", 2 * KD), signal("sq_used", 2 * KD, 2)
    ssum, ssum_p, root = signal("ssum", 4), signal("ssum_p", 4), signal("root", 4)
    scaled, affine, h_tile = signal("scaled", 2 * KD), signal("affine", 2 * KD), signal("h_tile", 3 * KD)
    cqn, ckvn = signal("cqn", 1), signal("ckvn", 1)
    lat_T, lat_ev, lat_out = signal("lat_T", 5), signal("lat_ev", 5), signal("lat_out", 32)
    last_ready, last_T, last_ev, last_out = signal("last_ready", 1), signal("last_T", 1), signal("last_ev", 1), signal("last_out", 32)
    y_ready, q_roped, gated = signal("y_ready", 4), signal("q_roped", 1), signal("gated", KD, 2)
    qlat_p, qlat_ev, qrs_ready = signal("qlat_p", 1), signal("qlat_ev", 1), signal("qrs_ready", 1)
    q_asm, k_asm, v_asm = signal("q_asm", NH), signal("k_asm", NH), signal("v_asm", NH)
    qk, smax, expd, normed = signal("qk", 4 * NH), signal("smax", 4 * NH), signal("expd", 4 * NH), signal("normed", NH)
    pt_p, pt_ev, pv, o_done = signal("pt_p", NH), signal("pt_ev", NH, 1), signal("pv", NH), signal("o_done", NH, 1)
    new_in = [signal(f"new_in{s}", NB // 2 * 16) for s in range(2)]
    pages_in = [[signal(f"pages_in{s}{g}", NB // 2 * 16 * 4) for g in range(4)] for s in range(2)]
    wuv_in, qst_ready = signal("wuv_in", 16), signal("qst_ready", NB)
    kt_p, kt_d, kt_a = signal("kt_p", 4 * NB), signal("kt_d", 4 * NB, 1), signal("kt_a", 4 * NB, 1)
    s_p, s_d, s_a = signal("s_p", 5 * NB), signal("s_d", 5 * NB), signal("s_a", 5 * NB, 1)
    s_max, s_exp = signal("s_max", NB), signal("s_exp", NB)
    spt_p, spt_a, spt_d = signal("spt_p", 5 * NB), signal("spt_a", 2 * NB), signal("spt_d", 3 * NB, 1)
    spv, so_d, so_T, so_a = signal("spv", NB, 2), signal("so_d", NB), signal("so_T", NB), signal("so_a", NB, 1)
    uvs, x_tile = signal("uvs", 1), signal("x_tile", KD)
    z_in, zconv, silud, prod = signal("z_in", 44), signal("zconv", 44, 2), signal("silud", KF), signal("prod", KF)
    act_hi_done, act_ready = signal("act_hi_done", KF), signal("act_ready", KF, 1)
    cl_T, cl_ev = signal("cl_T", 11), signal("cl_ev", 11, 1)
    cl_out = signal("cl_out", 32)
    x_new = signal("x_new", 1, 1)

    passed = [nc.alloc_semaphore(f"passed_{e}") for e in ("sp", "act", "dve", "pe", "pool")]

    def two(ap):
        return ap.rearrange("p (a b) -> p a b", a=2)

    def bank_pair(j):
        return PS[:, 2 * (j % 2):2 * (j % 2) + 2, 0:HT]

    with nc.Block() as block:

        @block.sync
        def _(sp):
            sp.dma_start(rows_in[:, 0:4, :], A["x_prompt"][0].rearrange("(n p) d -> p n d", p=128)).then_inc(x_in.sem, 16)
            sp.dma_start(rows_in[0:TS, 4, :], A["x_sample"].rearrange("b s d -> (b s) d")).then_inc(x_in.sem, 16)
            for dst, src in ((ident, "ident"), (ones, "ones"), (causal, "causal"), (causal_s, "causal_s")):
                sp.dma_start(dst[:], A[src]).then_inc(const_in.sem, 16)
            sp.dma_start(ramp[:].rearrange("p a b -> p (a b)"), A["ramp"]).then_inc(const_in.sem, 16)
            sp.dma_start(c_rows[0:1, :], A["c_prompt"]).then_inc(const_in.sem, 16)
            sp.dma_start(c_rows[1:NC, :], A["c_sample"]).then_inc(const_in.sem, 16)
            sp.dma_start(gf_rows[:], A["g_final"].rearrange("(n p) -> n p", p=128)).then_inc(const_in.sem, 16)
            sp.dma_start(tab[:], A["page_table"].rearrange("b n -> (b n)").rearrange("(o n) -> o n", o=1)).then_inc(tab_in.sem, 16)

            def unit(l, u, slot, dst, src):
                sp.wait_ge(lo_ready.sem, lo_ready.at(l, u - 1))
                sp.dma_start(dst, src).then_inc(loaded[slot].sem, 16)

            def square(l, w, u0, n, col0):
                with sp.Fori(0, n // 2) as i:
                    for s in range(2):
                        unit(l, u0 + 2 * i + s, s, raw[:, s].rearrange("p (k n) -> p k n", k=8),
                             w[bass.ds(l, 1), :, bass.ds(col0 + 256 * i + 128 * s, 128)]
                             .rearrange("a (k p) n -> p (a k) n", p=128))

            sp.wait_ge(tab_in.sem, 16)
            with sp.Fori(0, DEPTH) as l:
                def conditioning(i):
                    for s in range(6):
                        sp.wait_ge(ada_used.sem, ada_used.at(l, 6 * i + (s - 5)))
                        sp.dma_start(ada_w[:, s].rearrange("p (k n) -> p k n", k=8),
                                     A["w_ada"][bass.ds(l, 1), :, bass.ds(768 * i + 128 * s, 128)]
                                     .rearrange("a (k p) n -> p (a k) n", p=128)).then_inc(ada_in[s].sem, 16)

                sp.wait_ge(unit_used.sem, unit_used.at(l, 0))
                conditioning(0)
                sp.wait_ge(x_new.sem, x_new.at(l, 0))
                for r, (name, n) in zip((P_GA, P_GF, P_PS, P_BA, P_GQ, P_GK), (("g_attn", 8), ("g_ffn", 8), ("pool_scale", 8), ("b_ada", 48), ("g_q", 6), ("g_kv", 2))):
                    sp.dma_start(rows[r:r + n, 0, :], A[name][bass.ds(l, 1)].rearrange("a (n p) -> (a n) p", p=128)).then_inc(par_in.sem, 16)
                wc = A["w_conv"][bass.ds(l, 1)].rearrange("a c (n p) -> (a c n) p", p=128)
                sp.dma_start(rows[0:88, 1, :], wc[0:88]).then_inc(par_in.sem, 16)
                sp.dma_start(rows[0:44, 2, :], wc[88:132]).then_inc(par_in.sem, 16)
                sp.dma_start(rows[44:88, 2, :], A["b_conv"][bass.ds(l, 1)].rearrange("a (n p) -> (a n) p", p=128)).then_inc(par_in.sem, 16)
                scv = A["state_conv"][bass.ds(l, 1)].rearrange("a b r (n p) -> (a b r n) p", p=128)
                sp.dma_start(rows[:, 3:8, :], scv[0:640].rearrange("(c r) p -> r c p", r=128)).then_inc(par_in.sem, 16)
                sp.dma_start(rows[0:64, 8, :], scv[640:704]).then_inc(par_in.sem, 16)
                spl = A["state_pool"][bass.ds(l, 1)].rearrange("a b r (n p) -> (a b r n) p", p=128)
                sp.dma_start(rows[:, 9:16, :], spl[0:896].rearrange("(c r) p -> r c p", r=128)).then_inc(par_in.sem, 16)
                sp.dma_start(rows[0:64, 16, :], spl[896:960]).then_inc(par_in.sem, 16)
                sp.dma_start(rope[:].rearrange("p a b -> p (a b)"), A["rope"]).then_inc(rope_in.sem, 16)
                with sp.Fori(1, ADA // 6) as i:
                    conditioning(i)
                sp.wait_ge(ada_used.sem, ada_used.at(l, ADA))
                sp.sem_inc(passed[0], 1)
                square(l, A["w_in"], U_CQ, 8, 0)
                for s in range(2):
                    unit(l, U_KR + s, s, raw[:, s, 0:128].rearrange("p (k n) -> p k n", k=4),
                         A["w_in"][bass.ds(l, 1), 512 * s:512 * s + 512, C_KR:C_KR + DR].rearrange("a (k p) n -> p (a k) n", p=128))
                square(l, A["w_in"], U_U, 8, C_U)
                w_uq = A["w_uq"].rearrange("a (k p) (h n) -> p a k h n", p=128, n=DN + DR)
                with sp.Fori(0, 4) as i:
                    for s in range(2):
                        dst = raw[:, s, 0:768].rearrange("p (k h n) -> p k h n", k=KQ, h=2)
                        sp.wait_ge(lo_ready.sem, lo_ready.at(l, U_QN + 2 * i + s - 1))
                        for j in range(2):
                            sp.dma_start(dst[:, :, j, :], w_uq[:, bass.ds(l, 1), :, bass.ds(4 * i + 2 * s + j, 1), 0:DN]
                                         .rearrange("p a k h n -> p (a k) (h n)")).then_inc(loaded[s].sem, 16)
                with sp.Fori(0, 2) as i:
                    for s in range(2):
                        dst = raw[:, s, 0:768].rearrange("p (k h n) -> p k h n", k=KQ, h=4)
                        sp.wait_ge(lo_ready.sem, lo_ready.at(l, U_QR + 2 * i + s - 1))
                        for j in range(4):
                            sp.dma_start(dst[:, :, j, :], w_uq[:, bass.ds(l, 1), :, bass.ds(8 * i + 4 * s + j, 1), DN:DN + DR]
                                         .rearrange("p a k h n -> p (a k) (h n)")).then_inc(loaded[s].sem, 16)
                for g in range(4):
                    u = U_POOL + 3 * g
                    unit(l, u, u % 2, raw[:, u % 2, 0:512].rearrange("p (k n) -> p k n", k=2),
                         A["w_pool"][bass.ds(l, 1), g].rearrange("a (k p) n -> p (a k) n", p=128))
                    for e in range(2):
                        c = C_G + 128 * (2 * g + e)
                        unit(l, u + 1 + e, (u + 1 + e) % 2, raw[:, (u + 1 + e) % 2].rearrange("p (k n) -> p k n", k=8),
                             A["w_in"][bass.ds(l, 1), :, c:c + 128].rearrange("a (k p) n -> p (a k) n", p=128))
                square(l, A["w_in"], U_GB, 8, C_G + D)
                for w, u0 in ((A["w_uk"], U_UK), (A["w_uv"], U_UV)):
                    for s in range(2):
                        unit(l, u0 + s, s, raw[:, s].rearrange("p (k n) -> p k n", k=2),
                             w[bass.ds(l, 1)].rearrange("a (k p) h n -> p (a k) (h n)", p=128)[:, :, 512 * s:512 * s + 512])
                wo = A["w_out"]
                for s in range(2):
                    unit(l, U_OUT + s, s, raw[:, s].rearrange("p (k n) -> p k n", k=8),
                         wo[bass.ds(l, 1), :, 128 * s:128 * s + 128].rearrange("a (k p) n -> p (a k) n", p=128))
                def keys_of(i, s):
                    sp.dma_start(newk[:, s, :], O["lat_s"][bass.ds(l, 1), bass.ds(2 * i + s, 1)].rearrange("a b s c -> (a b s) c")).then_inc(new_in[s].sem, 16)
                    for j in range(NPG):
                        page = sp.value_load(tab[0:1, bass.ds((2 * i + s) * NPG + j, 1)], min_val=0, max_val=A["cache_latent"].shape[1] - 1)
                        sp.dma_start(pages[s][:, j, :], A["cache_latent"][bass.ds(l, 1), bass.ds(page, 1)].rearrange("a b k c -> (a b k) c")).then_inc(pages_in[s][j // 4].sem, 16)

                sp.wait_ge(lat_out.sem, lat_out.at(l, 32))
                sp.wait_ge(qlat_p.sem, qlat_p.at(l, 1))
                sp.wait_ge(q_asm.sem, q_asm.at(l, NH))
                sp.wait_ge(k_asm.sem, k_asm.at(l, NH))
                keys_of(0, 0)
                sp.wait_ge(v_asm.sem, v_asm.at(l, NH))
                keys_of(0, 1)
                with sp.Fori(1, NB // 2) as i:
                    for s in range(2):
                        sp.wait_ge(spv.sem, spv.at(l, 2 * i + s - 1))
                        keys_of(i, s)
                sp.dma_start(wuv[:], A["w_uv"][bass.ds(l, 1)].rearrange("a (k p) h n -> p (a k) (h n)", p=128)).then_inc(wuv_in.sem, 16)
                with sp.Fori(1, 4) as i:
                    for s in range(2):
                        unit(l, U_OUT + 2 * i + s, s, raw[:, s].rearrange("p (k n) -> p k n", k=8),
                             wo[bass.ds(l, 1), :, bass.ds(256 * i + 128 * s, 128)].rearrange("a (k p) n -> p (a k) n", p=128))
                with sp.Fori(0, KF) as j:
                    for s in range(2):
                        unit(l, U_UP + 2 * j + s, s, raw[:, s].rearrange("p (k n) -> p k n", k=8),
                             A["w_up"][bass.ds(l, 1), :, bass.ds(DF * s + 128 * j, 128)].rearrange("a (k p) n -> p (a k) n", p=128))
                with sp.Fori(0, 4) as i:
                    for v in range(6):
                        kk = 8 if v % 3 < 2 else KF - 16
                        r0 = 1024 * (v % 3)
                        unit(l, U_DOWN + 6 * i + v, v % 2, raw[:, v % 2, 0:128 * kk].rearrange("p (k n) -> p k n", k=kk),
                             A["w_down"][bass.ds(l, 1), r0:r0 + 128 * kk, bass.ds(256 * i + 128 * (v // 3), 128)]
                             .rearrange("a (k p) n -> p (a k) n", p=128))

        @block.scalar
        def _(act):
            def hi(l, u, i, slot):
                pieces = loads_before(u + 4) - loads_before(u + 2) if not isinstance(i, int) else 0
                act.wait_ge(loaded[slot].sem, 16 * (l * LOADS + loads_before(u + 2) + pieces * i))
                act.wait_ge(unit_used.sem, unit_used.at(l, u + 2 * i - 1))
                nc.scalar.activation(whi[:, slot], raw[:, slot], ACT.Copy).then_inc(hi_ready.sem, 1)

            for phase in ("qkv", "u", "uq", "g", "uk", "uv", "up"):
                act.sem_inc(free[phase].sem, 2)
            for readout in (pt_ev, kt_a, s_a, so_a, cl_ev):
                act.sem_inc(readout.sem, 1)
            for f in range(KD):
                act.wait_ge(start_T.sem, f + 1)
                b = 2 * (f % 2)
                nc.scalar.activation(x[:, f, 0:TP], PS[:, b, 0:TP], ACT.Copy)
                nc.scalar.activation(x[:, f, TP:T], PS[:, b + 1, 0:TS], ACT.Copy).then_inc(start_ev.sem, 1)
            act.wait_ge(start_T.sem, KD + 1)
            nc.scalar.activation(cond[:].rearrange("p a b -> p (a b)"), PS[:, 4, 0:KD * NC], ACT.Copy)
            nc.scalar.activation(g_fin[:], PS[:, 4, 128:128 + KD], ACT.Copy)
            nc.scalar.activation(ident_r[:], ident[:], ACT.Copy)
            nc.scalar.drain().then_inc(cond_ready.sem, 1)
            act.wait_ge(eps_set.sem, 1)

            def norm_squares(l):
                with act.Fori(0, KD // 2) as i:
                    for s in range(2):
                        act.wait_ge(sq_used.sem, sq_used.at(l, 2 * i + s - 1))
                        nc.scalar.activation(tmp[:, s, :], x[:, bass.ds(2 * i + s, 1), :].rearrange("p a b -> p (a b)"), ACT.Square).then_inc(sq.sem, 1)

            def root_of(l, k, n):
                act.wait_ge(ssum_p.sem, ssum_p.at(l, k + 1))
                nc.scalar.activation(two(kv_sum[:, 1, :] if k == 2 else rinv[:]), PS[:, (0 if k == 0 else 6):(2 if k == 0 else 8), 0:HT], ACT.Sqrt, bias=eps[:, 0:1], scale=1.0 / n).then_inc(root.sem, 1)

            def norm_affine(l, k, gain, shift):
                with act.Fori(0, KD // 2) as i:
                    for s in range(2):
                        act.wait_ge(scaled.sem, scaled.at(l, KD * k + 2 * i + s + 1))
                        nc.scalar.activation(tmp[:, s, 0:TP], tmp[:, s, 0:TP], ACT.Identity,
                                             bias=mod[:, bass.ds(shift + 2 * i + s, 1), 0:1].rearrange("p a b -> p (a b)"),
                                             scale=gain[:, bass.ds(2 * i + s, 1), 0:1].rearrange("p a b -> p (a b)"))
                        nc.scalar.drain()
                        nc.scalar.activation(h_hi[:, bass.ds(2 * i + s, 1), :].rearrange("p a b -> p (a b)"), tmp[:, s, :], ACT.Copy).then_inc(affine.sem, 1)

            def tiles(l, u0, n, evac):
                def pair(i):
                    for s in range(2):
                        act.wait_ge(unit_used.sem, unit_used.at(l, 2 * i + (u0 + s + 1)))
                        hi(l, u0 + s + 2 + (2 * i if isinstance(i, int) else 0), 0 if isinstance(i, int) else i, s)
                        evac(2 * i + s, s)

                if n > 2:
                    with act.Fori(0, n // 2 - 1) as i:
                        pair(i)
                pair(n // 2 - 1)

            def tile_of(t, f):
                return two(t[:, bass.ds(f, 1), :].rearrange("p a b -> p (a b)"))

            with act.Fori(0, DEPTH) as l:
                norm_squares(l)
                root_of(l, 0, D)
                act.wait_ge(par_T.sem, par_T.at(l, 1))
                nc.scalar.activation(par[:], PS[:, 0, 0:P_ALL], ACT.Copy)
                nc.scalar.activation(convp[:].rearrange("p a b -> p (a b)"), PS[:, 0, 80:256], ACT.Copy)
                cp = conv_prev[:].rearrange("p a b -> p (a b)")
                nc.scalar.activation(cp[:, 0:512], PS[:, 1, :], ACT.Copy)
                nc.scalar.activation(cp[:, 512:704], PS[:, 0, 256:448], ACT.Copy)
                pp = pool_prev[:].rearrange("p a b -> p (a b)")
                nc.scalar.activation(pp[:, 0:512], PS[:, 2, :], ACT.Copy)
                nc.scalar.activation(pp[:, 512:960], PS[:, 3, 0:448], ACT.Copy).then_inc(par_ev.sem, 1)
                act.wait_ge(ada_used.sem, ada_used.at(l, ADA))
                hi(l, 0, 0, 0)
                hi(l, 1, 0, 1)
                norm_affine(l, 0, gain1, 0)


                def to_cq(f, s):
                    nc.scalar.activation(tile_of(cq, f), bank_pair(s), ACT.Copy).then_inc(free["qkv"].sem, 1)

                def to_ckv(f, s):
                    nc.scalar.activation(tile_of(ckv, f), bank_pair(s), ACT.Copy).then_inc(free["qkv"].sem, 1)

                tiles(l, U_CQ, 6, to_cq)
                tiles(l, U_KV, 2, to_ckv)
                hi(l, U_KR + 2, 0, 0)
                act.wait_ge(unit_used.sem, unit_used.at(l, U_KR + 2))
                nc.scalar.activation(two(krope[:]), PS[0:DR, 0:2, 0:HT], ACT.Copy).then_inc(free["qkv"].sem, 2)
                hi(l, U_KR + 3, 0, 1)


                def to_u(f, s):
                    b = 2 * s
                    ue = uext[:, bass.ds(f, 1), :].rearrange("p a b -> p (a b)")
                    nc.scalar.activation(ue[:, CTX:CTX + HT], PS[:, b, 0:HT], ACT.Copy)
                    nc.scalar.activation(ue[:, CTX + HT:US], PS[:, b + 1, 0:TP - HT], ACT.Copy)
                    nc.scalar.activation(ue[:, US:UE].rearrange("p (b c) -> p b c", b=NB)[:, :, CTX:], PS[:, b + 1, TP - HT:HT].rearrange("p (b c) -> p b c", b=NB),
                                         ACT.Copy).then_inc(free["u"].sem, 1)

                tiles(l, U_U, 4, to_u)
                root_of(l, 1, QL)
                root_of(l, 2, KVL)
                tiles(l, U_U + 4, 4, lambda f, s: to_u(f + 4, s))
                for n in range(5):
                    act.wait_ge(lat_T.sem, lat_T.at(l, n + 1))
                    m = 128 if n < 4 else TS
                    nc.scalar.activation(lat_rows[0:m, n, :], PS[0:m, 4 + n % 2, 0:LAT], ACT.Copy).then_inc(lat_ev.sem, 1)
                act.wait_ge(lat_ev.sem, lat_ev.at(l, 5))
                act.dma_start(O["lat_p"][bass.ds(l, 1)].rearrange("a b (n p) c -> p (a b n) c", p=128), lat_rows[:, 0:4, :]).then_inc(lat_out.sem, 16)
                act.dma_start(O["lat_s"][bass.ds(l, 1)].rearrange("a b s c -> (a b s) c"), lat_rows[0:TS, 4, :]).then_inc(lat_out.sem, 16)
                act.wait_ge(last_T.sem, last_T.at(l, 1))
                nc.scalar.activation(pool_rows[0:120, 0], PS[0:120, 4:6, :], ACT.Copy)
                nc.scalar.activation(pool_rows[0:CTX, 1], PS[0:CTX, 6:8, :], ACT.Copy).then_inc(last_ev.sem, 1)
                act.wait_ge(last_ev.sem, last_ev.at(l, 1))
                act.dma_start(O["pool_s"][bass.ds(l, 1)].rearrange("a b r d -> (a b r) d"), pool_rows[0:120, 0].rearrange("p a b -> p (a b)")).then_inc(last_out.sem, 16)
                act.dma_start(O["pool_p"][bass.ds(l, 1)].rearrange("a b r d -> (a b r) d"), pool_rows[0:CTX, 1].rearrange("p a b -> p (a b)")).then_inc(last_out.sem, 16)

                act.wait_ge(last_out.sem, last_out.at(l, 32))
                act.wait_ge(lat_out.sem, lat_out.at(l, 32))

                def to_qn(f, s):
                    nc.scalar.activation(tile_of(qn, f), bank_pair(s), ACT.Copy).then_inc(free["uq"].sem, 1)

                def to_qr(f, s):
                    nc.scalar.activation(tile_of(qr, f), bank_pair(s), ACT.Copy).then_inc(free["uq"].sem, 1)

                tiles(l, U_QN, 8, to_qn)
                tiles(l, U_QR, 4, to_qr)

                for g in range(4):
                    u = U_POOL + 3 * g
                    hi(l, u + 2, 0, u % 2)
                    for e in range(2):
                        act.wait_ge(unit_used.sem, unit_used.at(l, u + 2 + e))
                        act.wait_ge(gated.sem, gated.at(l, 2 * g + e - 1))
                        nc.scalar.activation(two(gate_a[:, e, :]), bank_pair(e), ACT.Sigmoid).then_inc(free["g"].sem, 1)
                        hi(l, u + 3 + e, 0, (u + 1 + e) % 2)

                def to_gate_b(f, s):
                    nc.scalar.activation(tile_of(gate_b, f), bank_pair(s), ACT.Sigmoid).then_inc(free["g"].sem, 1)

                tiles(l, U_GB, 8, to_gate_b)

                for p in range(8):
                    act.wait_ge(full["uk"].sem, full["uk"].at(l, p + 1))
                    nc.scalar.activation(kn[:, p, :], PS[:, 2 * (p % 2), :], ACT.Copy)
                    nc.scalar.activation(wukT[:, p, :], PS[:, 2 * (p % 2) + 1, 0:KVL], ACT.Copy).then_inc(free["uk"].sem, 1)
                    if p % 4 == 3:
                        hi(l, U_UK + p // 4 + 2, 0, p // 4)
                for n in range(4):
                    act.wait_ge(full["uv"].sem, full["uv"].at(l, n + 1))
                    nc.scalar.activation(vn[:, 2 * (n % 2):2 * (n % 2) + 2, 512 * (n // 2):512 * (n // 2) + 512], PS[:, 2 * (n % 2):2 * (n % 2) + 2, :], ACT.Copy).then_inc(free["uv"].sem, 1)
                    if n % 2 == 1:
                        hi(l, U_UV + n // 2 + 2, 0, n // 2)
                act.wait_ge(qlat_p.sem, qlat_p.at(l, 1))
                for c in range(KC):
                    for g in range(2):
                        for h8 in range(8):
                            last = nc.scalar.activation(qlat[:, c, :, 2 * h8 + g, :], PS[:, 4 + 2 * c + g, 64 * h8:64 * h8 + 64].rearrange("p (b s) -> p b s", b=NB), ACT.Copy)

                last.then_inc(qlat_ev.sem, 1)

                def prompt_head(i, j):
                    h = 4 * i + j
                    for qb in range(4):
                        act.wait_ge(smax.sem, smax.at(l, 4 * h + qb + 1))
                        o = 64 * qb * (qb + 1)
                        nc.scalar.activation(prob[:, o:o + 128 * (qb + 1)], PS[:, qb, 0:128 * (qb + 1)], ACT.Exp,
                                             bias=softm[:, 4 + qb:5 + qb], scale=SCALE, accum_out=softm[:, 8 + qb:9 + qb]).then_inc(expd.sem, 1)
                    act.wait_ge(pt_p.sem, pt_p.at(l, h + 1))
                    nc.scalar.activation(probT[:, 0:512], PS[:, 4, :], ACT.Copy)
                    nc.scalar.activation(probT[:, 512:896], PS[:, 5, 0:384], ACT.Copy)
                    nc.scalar.activation(probT[:, 896:1280], PS[:, 6, 0:384], ACT.Copy).then_inc(pt_ev.sem, 1)

                def head_query(p, s):
                    nc.scalar.activation(q96[0:DN, s, :], qn[64 * s:64 * s + 64, bass.ds(p, 1), 0:TP].rearrange("p a b -> p (a b)"),
                                         ACT.Copy).then_inc(q_asm.sem, 1)

                head_query(0, 0)
                head_query(0, 1)
                with act.Fori(0, 3) as i:
                    for j in range(4):
                        prompt_head(i, j)
                        head_query(2 * i + (j // 2 + 1), j % 2)
                for j in range(4):
                    prompt_head(3, j)
                    if j < 2:
                        head_query(7, j)

                def keys(b, g):
                    act.wait_ge(kt_p.sem, kt_p.at(l, 4 * b + (g + 1)))
                    nc.scalar.activation(keysT[g % 2][:, 1, :], PS[:, 1, :], ACT.Copy).then_inc(kt_a.sem, 1)

                def scores(b, g):
                    act.wait_ge(s_d.sem, s_d.at(l, 5 * b + (g + 1)))
                    w = 512 if g < 4 else NS
                    nc.scalar.activation(sc[:, 512 * g:512 * g + w], PS[:, 3 + g % 2, 0:w], ACT.Copy).then_inc(s_a.sem, 1)

                def latent_output(b):
                    act.wait_ge(so_T.sem, so_T.at(l, b + 1))
                    for c in range(KC):
                        last = nc.scalar.activation(olatT[:, c, :, bass.ds(b, 1), :].rearrange("p h b s -> p h (b s)"),
                                                    PS[:, 7, 256 + 128 * c:384 + 128 * c].rearrange("p (h s) -> p h s", h=NH), ACT.Copy)
                    last.then_inc(so_a.sem, 1)

                def sequence(b, first=False, last=False):
                    for g in range(4):
                        if g < 3:
                            keys(b, g + 1)
                        scores(b, g)
                        if g == 0 and not first:
                            latent_output(b - 1)
                    scores(b, 4)
                    nc.scalar.drain()
                    act.wait_ge(s_max.sem, s_max.at(l, b + 1))
                    nc.scalar.activation(sc[:], sc[:], ACT.Exp, bias=softm[:, 24:25], scale=SCALE, accum_out=softm[:, 25:26]).then_inc(s_exp.sem, 1)
                    if not last:
                        keys(b + 1, 0)
                    for g in (0, 2):
                        act.wait_ge(spt_p.sem, spt_p.at(l, 5 * b + g + 1))
                        nc.scalar.activation(pT[:, 4 * g:4 * g + 4, :].rearrange("p a b -> p (a b)"), PS[:, 5 + g % 2, :], ACT.Copy).then_inc(spt_a.sem, 1)

                keys(0, 0)
                sequence(0, first=True)
                sequence(1)
                with act.Fori(1, NB // 2 - 1) as i:
                    sequence(2 * i)
                    sequence(2 * i + 1)
                sequence(NB - 2)
                sequence(NB - 1, last=True)
                latent_output(NB - 1)

                with act.Fori(0, KD // 2) as i:
                    for s in range(2):
                        hi(l, U_OUT + 2 + s, i, s)
                        act.wait_ge(x_tile.sem, x_tile.at(l, 2 * i + s + 1))
                        act.wait_ge(sq_used.sem, sq_used.at(l, KD + 2 * i + s - 1))
                        nc.scalar.activation(tmp[:, s, :], x[:, bass.ds(2 * i + s, 1), :].rearrange("p a b -> p (a b)"), ACT.Square).then_inc(sq.sem, 1)
                root_of(l, 3, D)
                norm_affine(l, 1, gain2, 24)

                def up_tile(j, s):
                    b = 2 * s
                    f = j + KF * s
                    nc.scalar.drain()
                    if isinstance(j, int):
                        hi(l, U_UP + 2 * j + s + 2, 0, s)
                    else:
                        hi(l, U_UP + s + 2, j, s)
                    act.wait_ge(unit_used.sem, unit_used.at(l, 2 * j + (U_UP + s + 1)))
                    act.wait_ge(zconv.sem, zconv.at(l, 2 * j + (s - 1)))
                    zs = zext[:, s, ZS:ZE].rearrange("p (b c) -> p b c", b=NB)
                    nc.scalar.activation(zext[:, s, 2:2 + HT], PS[:, b, 0:HT], ACT.Copy)
                    nc.scalar.activation(zext[:, s, 2 + HT:ZS], PS[:, b + 1, 0:TP - HT], ACT.Copy)
                    nc.scalar.activation(zs[:, :, 2:], PS[:, b + 1, TP - HT:HT].rearrange("p (b c) -> p b c", b=NB), ACT.Copy).then_inc(free["up"].sem, 1)
                    prev = conv_prev[:, :, bass.ds(f, 1)].rearrange("p (b r) o -> p b (r o)", b=NB)
                    nc.scalar.activation(zs[:, :, 0:2], prev, ACT.Copy)
                    nc.scalar.drain().then_inc(z_in.sem, 1)
                    cl = conv_last[:, bass.ds(f, 1), :].rearrange("p a b -> p (a b)")
                    nc.scalar.activation(cl[:, 0:2], zext[:, s, TP:ZS], ACT.Copy)
                    nc.scalar.activation(cl[:, 2:].rearrange("p (b r) -> p b r", b=NB), zs[:, :, NS:], ACT.Copy)

                def silu(j, buf):
                    act.wait_ge(zconv.sem, zconv.at(l, 2 * j + 1))
                    nc.scalar.activation(conv[buf][0][:, 0:ZE - 2], conv[buf][0][:, 0:ZE - 2], ACT.Silu).then_inc(silud.sem, 1)

                def act_parts(j, buf):
                    act.wait_ge(prod.sem, prod.at(l, j + 1))
                    ah = act_hi[:, bass.ds(j, 1), :].rearrange("p a b -> p (a b)")
                    nc.scalar.activation(ah[:, 0:TP], conv[buf][0][:, 0:TP], ACT.Copy)
                    nc.scalar.activation(ah[:, TP:T].rearrange("p (b c) -> p b c", b=NB), conv[buf][0][:, ZS:ZE].rearrange("p (b c) -> p b c", b=NB)[:, :, 0:NS],
                                         ACT.Copy).then_inc(act_hi_done.sem, 1)

                def up_pair(j, buf):
                    up_tile(j, 0)
                    silu(j - 1, 1 - buf)
                    up_tile(j, 1)
                    act_parts(j - 1, 1 - buf)

                up_tile(0, 0)
                up_tile(0, 1)
                with act.Fori(0, KF // 2 - 1) as i:
                    up_pair(2 * i + 1, 1)
                    up_pair(2 * i + 2, 0)
                up_pair(KF - 1, 1)
                silu(KF - 1, 1)
                act_parts(KF - 1, 1)
                for n in range(11):
                    act.wait_ge(cl_T.sem, cl_T.at(l, n + 1))
                    nc.scalar.activation(conv_rows[:, 512 * n:512 * n + 512], PS[0:2 * NC, 4 + n % 4, :], ACT.Copy).then_inc(cl_ev.sem, 1)
                act.wait_ge(cl_ev.sem, cl_ev.at(l, 11))
                act.dma_start(O["conv_p"][bass.ds(l, 1)].rearrange("a b r d -> (a b r) d"), conv_rows[0:2, :]).then_inc(cl_out.sem, 16)
                act.dma_start(O["conv_s"][bass.ds(l, 1)].rearrange("a b r d -> (a b r) d"), conv_rows[2:2 * NC, :]).then_inc(cl_out.sem, 16)
                with act.Fori(0, 11) as i:
                    hi(l, U_DOWN + 2, i, 0)
                    hi(l, U_DOWN + 3, i, 1)
                act.wait_ge(cl_out.sem, cl_out.at(l, 32))
                act.sem_inc(passed[1], 1)

            norm_squares(DEPTH)
            root_of(DEPTH, 0, D)
            for n in range(5):
                m = 128 if n < 4 else TS
                act.wait_ge(fin_T.sem, n + 1)
                if n >= 2:
                    act.wait_ge(y_out[n % 2].sem, 16 * (n // 2))
                nc.scalar.activation(y_rows[0:m, n % 2, :].rearrange("p (a b) -> p a b", a=2), PS[0:m, 2 * (n % 2):2 * (n % 2) + 2, :], ACT.Copy).then_inc(fin_ev.sem, 1)
                act.wait_ge(fin_ev.sem, n + 1)
                dst = O["y_p"][0, 128 * n:128 * n + 128, :] if n < 4 else O["y_s"].rearrange("b s d -> (b s) d")
                act.dma_start(dst, y_rows[0:m, n % 2, :]).then_inc(y_out[n % 2].sem, 16)
            act.wait_ge(y_out[0].sem, 48)
            act.wait_ge(y_out[1].sem, 32)
            act.wait_ge(lat_out.sem, lat_out.at(DEPTH, 0))
            act.wait_ge(last_out.sem, last_out.at(DEPTH, 0))

        @block.gpsimd
        def _(pool):
            pool.sem_inc(lo_ready.sem, 2)

            def lo(l, u, slot):
                pool.wait_ge(hi_ready.sem, hi_ready.at(l, u + 1))
                nc.gpsimd.tensor_tensor(wlo[:, slot], raw[:, slot], whi[:, slot].bitcast(F32), ALU.subtract).then_inc(lo_ready.sem, 1)

            def head_parts(p, s, j):
                pool.sem_inc(passed[4], 1)
                nc.gpsimd.tensor_copy(q96[DN:96, s, :], qr[32 * j:32 * j + 32, bass.ds(p[0], 1), 0:TP].rearrange("p a b -> p (a b)"))
                nc.gpsimd.drain()
                nc.gpsimd.tensor_copy(k96[0:DN, s, :], kn[64 * s:64 * s + 64, bass.ds(p[1], 1), :].rearrange("p a b -> p (a b)")).then_inc(k_asm.sem, 1)

            with pool.Fori(0, DEPTH) as l:
                with pool.Fori(0, U_OUT // 2) as i:
                    lo(l, 2 * i, 0)
                    lo(l, 2 * i + 1, 1)
                lo(l, U_OUT, 0)
                lo(l, U_OUT + 1, 1)
                nc.gpsimd.drain()
                pool.wait_ge(free["uv"].sem, free["uv"].at(l, 4))
                pool.wait_ge(q_roped.sem, q_roped.at(l, 1))
                head_parts((0, 0), 0, 0)
                nc.gpsimd.drain()
                head_parts((0, 0), 1, 1)
                with pool.Fori(0, 3) as i:
                    for j in range(4):
                        nc.gpsimd.drain()
                        pool.wait_ge(qk.sem, qk.at(l, 16 * i + (4 * j + 4)))
                        head_parts((i + (j + 2) // 4, 2 * i + (j // 2 + 1)), j % 2, (j + 2) % 4)
                for j in range(2):
                    nc.gpsimd.drain()
                    pool.wait_ge(qk.sem, qk.at(l, 4 * (12 + j) + 4))
                    head_parts((3, 7), j, j + 2)
                nc.gpsimd.drain()
                with pool.Fori(0, (UNITS - U_OUT - 2) // 2) as i:
                    lo(l, U_OUT + 2 + 2 * i, 0)
                    lo(l, U_OUT + 3 + 2 * i, 1)

        @block.vector
        def _(dve):
            v = nc.vector

            def flat(ap):
                return ap.rearrange("p a b -> p (a b)")

            def by_seq(ap):
                return ap.rearrange("p (b c) -> p b c", b=NB)

            def over_tokens(ap):
                return ap.unsqueeze(2).broadcast_to([128, NB, NS])

            v.memset(eps[:], EPS).then_inc(eps_set.sem, 1)
            for g in (sq_used, gated, zconv, free["pool"], free["out"], free["down"]):
                dve.sem_inc(g.sem, 2)
            dve.sem_inc(ada_ev.sem, 3)
            for readout in (o_done, kt_d, spt_d, act_ready, x_new):
                dve.sem_inc(readout.sem, 1)

            def add_squares(l, k, f, s):
                if not (isinstance(f, int) and f == 0):
                    v.drain()
                dve.wait_ge(sq.sem, sq.at(l, f + (KD * k + 1)))
                if isinstance(f, int) and f == 0:
                    v.tensor_copy(sumsq[:], tmp[:, s, :]).then_inc(sq_used.sem, 1)
                else:
                    v.tensor_tensor(sumsq[:], sumsq[:], tmp[:, s, :], ALU.add).then_inc(sq_used.sem, 1)

            def sum_squares(l):
                add_squares(l, 0, 0, 0)
                add_squares(l, 0, 1, 1)
                with dve.Fori(1, KD // 2) as i:
                    add_squares(l, 0, 2 * i, 0)
                    add_squares(l, 0, 2 * i + 1, 1)
                v.drain().then_inc(ssum.sem, 1)

            def inverse_rms(l, sums):
                dve.wait_ge(root.sem, root.at(l, sums + 1))
                v.reciprocal(rinv[:], rinv[:])
                v.drain()

            def normalise(l, k, gain, shift):
                def scale(f, s):
                    v.tensor_tensor(tmp[:, s, :], flat(x[:, bass.ds(f, 1), :]), rinv[:], ALU.mult)
                    v.drain()
                    t = by_seq(tmp[:, s, TP:T])
                    v.tensor_tensor(t, t, over_tokens(flat(gain[:, bass.ds(f, 1), 1:NC])), ALU.mult)
                    v.drain()
                    v.tensor_tensor(t, t, over_tokens(flat(mod[:, bass.ds(f + shift, 1), 1:NC])), ALU.add).then_inc(scaled.sem, 1)

                def rest(f, s):
                    dve.wait_ge(affine.sem, affine.at(l, f + (KD * k + 1)))
                    v.tensor_tensor(flat(h_lo[:, bass.ds(f, 1), :]), tmp[:, s, :], flat(h_hi[:, bass.ds(f, 1), :]).bitcast(F32), ALU.subtract)
                    v.drain().then_inc(h_tile.sem, 1)

                scale(0, 0)
                with dve.Fori(0, KD // 2 - 1) as i:
                    scale(2 * i + 1, 1)
                    rest(2 * i, 0)
                    scale(2 * i + 2, 0)
                    rest(2 * i + 1, 1)
                scale(KD - 1, 1)
                rest(KD - 2, 0)
                rest(KD - 1, 1)

            def residual(l, phase, gate, u0, units, m, s):
                dve.wait_ge(unit_used.sem, unit_used.at(l, u0 + units * (m + 1)))
                xm = flat(x[:, bass.ds(m, 1), :])
                g = mod[:, bass.ds(m + gate, 1), :].rearrange("p a b -> p (a b)")
                gated_s = rinv[:, TS * s:TS * s + TS]
                t = by_seq(gated_s)
                v.scalar_tensor_tensor(xm[:, 0:HT], PS[:, 2 * s, 0:HT], g[:, 0:1], xm[:, 0:HT], ALU.mult, ALU.add)
                v.scalar_tensor_tensor(xm[:, HT:TP], PS[:, 2 * s + 1, 0:TP - HT], g[:, 0:1], xm[:, HT:TP], ALU.mult, ALU.add)
                v.tensor_tensor(t, by_seq(PS[:, 2 * s + 1, TP - HT:HT]), over_tokens(g[:, 1:NC]), ALU.mult).then_inc(free[phase].sem, 1)
                v.drain()
                v.tensor_tensor(xm[:, TP:T], xm[:, TP:T], gated_s, ALU.add)

            with dve.Fori(0, DEPTH) as l:
                sum_squares(l)

                def ada_readout(i):
                    for g in range(3):
                        dve.wait_ge(ada_p.sem, ada_p.at(l, 3 * i + (g + 1)))
                        dve.wait_ge(ada_T.sem, ada_T.at(l, 3 * i + (g - 2)))
                        v.tensor_copy(ada_rows[:, g, :], PS[0:NC, (4, 5, 7)[g], 0:256]).then_inc(ada_ev.sem, 1)

                ada_readout(0)
                inverse_rms(l, 0)
                with dve.Fori(1, ADA // 6) as i:
                    ada_readout(i)
                dve.wait_ge(par_ev.sem, par_ev.at(l, 1))
                v.memset(uext[:, :, 0:CTX], 0.0)
                for b in range(NB):
                    o = US + b * (CTX + NS)
                    v.tensor_copy(uext[:, :, o:o + CTX], pool_prev[:, b * CTX:(b + 1) * CTX, :].rearrange("p r f -> p f r"))
                dve.wait_ge(ada_T.sem, ada_T.at(l, ADA // 2))
                v.tensor_tensor(mod[:], PS[:, 6, 0:48 * NC].rearrange("p (a b) -> p a b", a=48),
                                par[:, P_BA:P_GQ].unsqueeze(2).broadcast_to([128, 48, NC]), ALU.add)
                v.drain()
                v.scalar_tensor_tensor(gain1[:], mod[:, 8:16, :], 1.0, par[:, P_GA:P_GF].unsqueeze(2).broadcast_to([128, KD, NC]), ALU.add, ALU.mult)
                v.scalar_tensor_tensor(gain2[:], mod[:, 32:40, :], 1.0, par[:, P_GF:P_PS].unsqueeze(2).broadcast_to([128, KD, NC]), ALU.add, ALU.mult)
                v.drain()
                normalise(l, 0, gain1, 0)

                def latent_squares(src, n, dst, s0):
                    for f in range(n):
                        dve.wait_ge(free["qkv"].sem, free["qkv"].at(l, s0 + f + 1))
                        if f == 0:
                            v.tensor_tensor(dst, src[:, f, :], src[:, f, :], ALU.mult)
                        else:
                            v.tensor_tensor(tmp[:, 0, :], src[:, f, :], src[:, f, :], ALU.mult)
                            v.drain()
                            v.tensor_tensor(dst, dst, tmp[:, 0, :], ALU.add)
                        v.drain()
                    v.drain().then_inc(ssum.sem, 1)

                latent_squares(cq, KQ, sumsq[:], 0)
                latent_squares(ckv, KC, kv_sum[:, 0, :], KQ)
                dve.wait_ge(free["qkv"].sem, free["qkv"].at(l, 10))
                dve.wait_ge(rope_in.sem, rope_in.at(l, 16))
                dve.sem_inc(passed[2], 1)
                half_turn = [(j + 16) % 32 for j in range(32)]
                v.stream_shuffle(tmp[0:DR, 1, :], krope[:], mask=half_turn)
                v.drain()
                v.tensor_tensor(tmp[0:DR, 1, :], tmp[0:DR, 1, :], rope[0:DR, 1, :], ALU.mult)
                v.tensor_tensor(krope[:], krope[:], rope[0:DR, 0, :], ALU.mult)
                v.drain()
                v.tensor_tensor(krope[:], krope[:], tmp[0:DR, 1, :], ALU.add)
                dve.wait_ge(root.sem, root.at(l, 2))
                v.reciprocal(rinv[:], rinv[:])
                v.drain()
                for f in range(KQ):
                    v.scalar_tensor_tensor(cq[:, f, :], cq[:, f, :], par[:, P_GQ + f:P_GQ + f + 1], rinv[:], ALU.mult, ALU.mult)
                    v.drain()
                    v.tensor_copy(cq_hi[:, f, :], cq[:, f, :])
                    v.drain()
                    v.tensor_tensor(cq_lo[:, f, :], cq[:, f, :], cq_hi[:, f, :].bitcast(F32), ALU.subtract)
                v.drain().then_inc(cqn.sem, 1)
                dve.wait_ge(root.sem, root.at(l, 3))
                v.reciprocal(kv_sum[:, 1, :], kv_sum[:, 1, :])
                v.drain()
                for f in range(KC):
                    v.scalar_tensor_tensor(ckv[:, f, :], ckv[:, f, :], par[:, P_GK + f:P_GK + f + 1], kv_sum[:, 1, :], ALU.mult, ALU.mult)
                    v.drain()
                    v.tensor_copy(ckv_hi[:, f, :], ckv[:, f, :])
                    v.drain()
                    v.tensor_tensor(ckv_lo[:, f, :], ckv[:, f, :], ckv_hi[:, f, :].bitcast(F32), ALU.subtract)
                v.drain().then_inc(ckvn.sem, 1)

                dve.wait_ge(free["u"].sem, free["u"].at(l, KD))
                v.tensor_copy(pool_last[:, :, 0:CTX], uext[:, :, US - CTX:US])
                for b in range(NB):
                    o = US + b * (CTX + NS) + NS
                    v.tensor_copy(pool_last[:, :, CTX * (b + 1):CTX * (b + 2)], uext[:, :, o:o + CTX])
                v.drain().then_inc(last_ready.sem, 1)

                def window_mean(g):
                    u = uext[:, 2 * g:2 * g + 2, :]
                    src, d = u, 1
                    for n in range(g + 1):
                        dst = win if (g - n) % 2 == 0 else win2[g]
                        v.tensor_tensor(dst[:, :, 2 * d - 1:], src[:, :, 2 * d - 1:], src[:, :, d - 1:UE - d], ALU.add)
                        v.drain()
                        src, d = dst, 2 * d
                    v.tensor_tensor(win[:, :, CTX:CTX + 15], win[:, :, CTX:CTX + 15], ramp[:, g:g + 1, 0:15].broadcast_to([128, 2, 15]), ALU.mult)
                    v.drain()
                    v.scalar_tensor_tensor(win[:, :, CTX:], win[:, :, CTX:], 1.0 / WINDOWS[g], u[:, :, CTX:], ALU.mult, ALU.subtract)
                    v.drain()

                    def parts(t):
                        yield t[:, :, 0:TP], win[:, :, CTX:US], slice(0, TP)
                        for e in range(2):
                            yield (t[:, e, TP:T].rearrange("p (b c) -> p b c", b=NB),
                                   win[:, e, US:UE].rearrange("p (b c) -> p b c", b=NB)[:, :, CTX:], e)

                    for out, val, _ in parts(y_hi[g]):
                        v.tensor_copy(out, val)
                    v.drain()
                    for (out, val, _), (part, _, _) in zip(parts(y_lo[g]), parts(y_hi[g])):
                        v.tensor_tensor(out, val, part.bitcast(F32), ALU.subtract)
                    v.drain().then_inc(y_ready.sem, 1)

                window_mean(0)
                dve.wait_ge(free["uq"].sem, free["uq"].at(l, 12))
                dve.sem_inc(passed[2], 1)
                for g in range(4):
                    if g < 3:
                        window_mean(g + 1)
                    for m in (2 * g, 2 * g + 1):
                        dve.wait_ge(full["pool"].sem, full["pool"].at(l, m + 1))
                        b = 4 + 2 * (m % 2)
                        v.tensor_scalar(two(uext[:, m, 0:T]), PS[:, b:b + 2, 0:HT], par[:, P_PS + m:P_PS + m + 1], None, ALU.mult).then_inc(free["pool"].sem, 1)
                    v.drain()
                    for m in (2 * g, 2 * g + 1):
                        dve.wait_ge(free["g"].sem, free["g"].at(l, m + 1))
                        v.tensor_tensor(uext[:, m, 0:T], uext[:, m, 0:T], gate_a[:, m % 2, :], ALU.mult).then_inc(gated.sem, 1)
                v.drain()
                for t in range(4):
                    v.stream_shuffle(tmp[:, 0, :], qr[:, t, :], mask=half_turn)
                    v.tensor_tensor(qr[:, t, :], qr[:, t, :], rope[:, 0, :], ALU.mult)
                    v.drain()
                    v.tensor_tensor(tmp[:, 0, :], tmp[:, 0, :], rope[:, 1, :], ALU.mult)
                    v.drain()
                    v.tensor_tensor(qr[:, t, :], qr[:, t, :], tmp[:, 0, :], ALU.add)
                    v.drain()
                v.drain().then_inc(q_roped.sem, 1)

                v.drain()
                dve.wait_ge(free["uv"].sem, free["uv"].at(l, 4))
                for s in range(2):
                    v.tensor_copy(k96[DN:96, s, :], krope[:, 0:TP])
                for j in range(4):
                    for t in range(4):
                        v.tensor_copy(qrs[:, :, 4 * t + j, :], by_seq(qr[32 * j:32 * j + 32, t, TP:T]))

                def out_head(p, s, n):
                    dve.wait_ge(pv.sem, pv.at(l, n))
                    gb = flat(gate_b[64 * s:64 * s + 64, bass.ds(p, 1), 0:TP])
                    v.tensor_tensor(gb, gb, PS[64 * s:64 * s + 64, 7, :], ALU.mult).then_inc(o_done.sem, 1)

                def prompt_head(i, j):
                    h = 4 * i + j
                    s = j % 2
                    if not isinstance(i, int) or h >= 2:
                        dve.wait_ge(pv.sem, pv.at(l, h - 1))
                    v.tensor_copy(v64[:, s], vn[:, :, bass.ds(DV * h, DV)]).then_inc(v_asm.sem, 1)
                    for qb in range(4):
                        dve.wait_ge(qk.sem, qk.at(l, 4 * h + (qb + 1)))
                        v.tensor_reduce(softm[:, qb:qb + 1], PS[:, qb, 0:128 * (qb + 1)], AX.X, ALU.max)
                        v.drain()
                        v.tensor_scalar(softm[:, 4 + qb:5 + qb], softm[:, qb:qb + 1], -SCALE, None, ALU.mult).then_inc(smax.sem, 1)
                    for qb in range(4):
                        dve.wait_ge(expd.sem, expd.at(l, 4 * h + (qb + 1)))
                        v.reciprocal(softm[:, 12 + qb:13 + qb], softm[:, 8 + qb:9 + qb])
                        v.drain()
                        o = 64 * qb * (qb + 1)
                        pr = prob[:, o:o + 128 * (qb + 1)]
                        v.tensor_scalar(pr, pr, softm[:, 12 + qb:13 + qb], None, ALU.mult)
                    v.drain().then_inc(normed.sem, 1)
                    if not isinstance(i, int) or h >= 1:
                        out_head(2 * i + (j - 1) // 2, (j - 1) % 2, h)

                for j in range(4):
                    prompt_head(0, j)
                with dve.Fori(1, 4) as i:
                    for j in range(4):
                        prompt_head(i, j)
                out_head(7, 1, 16)
                v.drain()

                dve.wait_ge(qlat_ev.sem, qlat_ev.at(l, 1))
                dve.sem_inc(passed[2], 1)
                def queries(b, s):
                    v.tensor_copy(qst[:, s, 0:2, :].rearrange("p c (h s) -> p c h s", h=NH), qlat[:, :, bass.ds(b, 1), :, :].rearrange("p c b h s -> p c (b h) s"))
                    v.tensor_copy(qst[0:DR, s, 2, :], qrs[:, bass.ds(b, 1), :, :].rearrange("p b h s -> p (b h s)")).then_inc(qst_ready.sem, 1)

                def keys(b, g):
                    dve.wait_ge(kt_p.sem, kt_p.at(l, 4 * b + (g + 1)))
                    v.tensor_copy(keysT[g % 2][:, 0, :], PS[:, 0, :])
                    v.tensor_copy(keysT[g % 2][0:DR, 2, :], PS[0:DR, 2, :]).then_inc(kt_d.sem, 1)

                def scores(b, g):
                    dve.wait_ge(s_p.sem, s_p.at(l, 5 * b + (g + 1)))
                    w = 512 if g < 4 else NS
                    if g == 4:
                        v.tensor_tensor(PS[:, 3, 0:w], PS[:, 3, 0:w], causal_s[:], ALU.add)
                        v.drain()
                    v.tensor_reduce(softm[:, 16 + g:17 + g], PS[:, 3 + g % 2, 0:w], AX.X, ALU.max).then_inc(s_d.sem, 1)

                def sequence(b, s, last=False):
                    for g in range(4):
                        if g < 3:
                            keys(b, g + 1)
                        scores(b, g)
                    scores(b, 4)
                    v.drain()
                    v.tensor_reduce(softm[:, 21:22], softm[:, 16:21], AX.X, ALU.max)
                    v.drain()
                    v.tensor_scalar(softm[:, 24:25], softm[:, 21:22], -SCALE, None, ALU.mult).then_inc(s_max.sem, 1)
                    if not last:
                        queries(b + 1, 1 - s)
                        keys(b + 1, 0)
                    dve.wait_ge(s_exp.sem, s_exp.at(l, b + 1))
                    v.reciprocal(softm[:, 26:27], softm[:, 25:26])
                    for g in (1, 3):
                        dve.wait_ge(spt_p.sem, spt_p.at(l, 5 * b + (g + 1)))
                        v.tensor_copy(pT[:, 4 * g:4 * g + 4, :].rearrange("p a b -> p (a b)"), PS[:, 6, :]).then_inc(spt_d.sem, 1)
                    dve.wait_ge(spt_p.sem, spt_p.at(l, 5 * b + 5))
                    v.tensor_copy(pT[0:NS, NPG, :], PS[0:NS, 5, 0:128]).then_inc(spt_d.sem, 1)
                    dve.wait_ge(spv.sem, spv.at(l, b + 1))
                    v.tensor_scalar(olat[:], PS[:, 7, 0:KVL], softm[:, 26:27], None, ALU.mult).then_inc(so_d.sem, 1)

                queries(0, 0)
                keys(0, 0)
                with dve.Fori(0, NB // 2 - 1) as i:
                    sequence(2 * i, 0)
                    sequence(2 * i + 1, 1)
                sequence(NB - 2, 0)
                sequence(NB - 1, 1, last=True)
                dve.wait_ge(uvs.sem, uvs.at(l, 1))
                v.tensor_tensor(gate_b[:, :, TP:T], gate_b[:, :, TP:T], PS[:, 0, :].rearrange("p (a b) -> p a b", a=KD), ALU.mult)
                v.drain()

                for f in range(KD):
                    s = f % 2
                    v.tensor_tensor(tmp[:, s, :], gate_b[:, f, :], uext[:, f, 0:T], ALU.add)
                    v.drain()
                    v.tensor_copy(h_hi[:, f, :], tmp[:, s, :])
                    v.drain()
                    v.tensor_tensor(h_lo[:, f, :], tmp[:, s, :], h_hi[:, f, :].bitcast(F32), ALU.subtract)
                    v.drain().then_inc(h_tile.sem, 1)
                def out_tile(m, s):
                    residual(l, "out", 16, U_OUT, 1, m, s)
                    v.drain().then_inc(x_tile.sem, 1)

                out_tile(0, 0)
                out_tile(1, 1)
                add_squares(l, 1, 0, 0)
                with dve.Fori(1, KD // 2) as i:
                    out_tile(2 * i, 0)
                    add_squares(l, 1, 2 * i - 1, 1)
                    out_tile(2 * i + 1, 1)
                    add_squares(l, 1, 2 * i, 0)
                add_squares(l, 1, KD - 1, 1)
                v.drain().then_inc(ssum.sem, 1)

                inverse_rms(l, 3)
                normalise(l, 1, gain2, 24)
                v.memset(zext[:, :, 0:2], 0.0)

                def convolve(j, s, buf):
                    f = j + KF * s
                    c = conv[buf][s][:, 0:ZE - 2]
                    v.drain()
                    dve.wait_ge(z_in.sem, z_in.at(l, 2 * j + (s + 1)))
                    v.tensor_scalar(c, zext[:, s, 2:ZE], convp[:, 1, bass.ds(f, 1)], convp[:, 1, bass.ds(f + 2 * KF, 1)], ALU.mult, ALU.add)
                    v.drain()
                    v.scalar_tensor_tensor(c, zext[:, s, 1:ZE - 1], convp[:, 0, bass.ds(f + 2 * KF, 1)], c, ALU.mult, ALU.add)
                    v.drain()
                    v.scalar_tensor_tensor(c, zext[:, s, 0:ZE - 2], convp[:, 0, bass.ds(f, 1)], c, ALU.mult, ALU.add).then_inc(zconv.sem, 1)

                def gate_value(j, buf):
                    v.drain()
                    dve.wait_ge(silud.sem, silud.at(l, j + 1))
                    v.tensor_tensor(conv[buf][0][:, 0:ZE - 2], conv[buf][0][:, 0:ZE - 2], conv[buf][1][:, 0:ZE - 2], ALU.mult).then_inc(prod.sem, 1)

                def act_rest(j, buf):
                    v.drain()
                    dve.wait_ge(act_hi_done.sem, act_hi_done.at(l, j + 1))
                    ah, al = flat(act_hi[:, bass.ds(j, 1), :]).bitcast(F32), flat(act_lo[:, bass.ds(j, 1), :])
                    v.tensor_tensor(al[:, 0:TP], conv[buf][0][:, 0:TP], ah[:, 0:TP], ALU.subtract)
                    v.tensor_tensor(by_seq(al[:, TP:T]), by_seq(conv[buf][0][:, ZS:ZE])[:, :, 0:NS], by_seq(ah[:, TP:T]), ALU.subtract).then_inc(act_ready.sem, 1)

                def up_pair(j, buf):
                    convolve(j, 0, buf)
                    gate_value(j - 1, 1 - buf)
                    convolve(j, 1, buf)
                    act_rest(j - 1, 1 - buf)

                convolve(0, 0, 0)
                convolve(0, 1, 0)
                with dve.Fori(0, KF // 2 - 1) as i:
                    up_pair(2 * i + 1, 1)
                    up_pair(2 * i + 2, 0)
                up_pair(KF - 1, 1)
                gate_value(KF - 1, 1)
                act_rest(KF - 1, 1)
                v.drain()
                with dve.Fori(0, KD // 2) as i:
                    residual(l, "down", 40, U_DOWN, 3, 2 * i, 0)
                    residual(l, "down", 40, U_DOWN, 3, 2 * i + 1, 1)
                v.drain().then_inc(x_new.sem, 1)

            sum_squares(DEPTH)
            dve.wait_ge(root.sem, root.at(DEPTH, 1))
            v.reciprocal(rinv[:], rinv[:])
            v.drain()
            for f in range(KD):
                v.scalar_tensor_tensor(yT[:, f, :], x[:, f, :], g_fin[:, f:f + 1], rinv[:], ALU.mult, ALU.mult)
            v.drain().then_inc(fin_norm.sem, 1)

        @block.tensor
        def _(pe):
            mm = nc.tensor.matmul
            pe.sem_inc(unit_used.sem, 2)
            pe.sem_inc(spv.sem, 2)
            pe.sem_inc(ada_T.sem, 3)
            pe.sem_inc(ada_used.sem, 6)

            def turn(out, src, k):
                return nc.tensor.transpose(out, src, ident[0:k, 0:k])

            pe.wait_ge(x_in.sem, 32)
            pe.wait_ge(const_in.sem, 16 * 8)
            for f in range(KD):
                if f >= 2:
                    pe.wait_ge(start_ev.sem, f - 1)
                for n in range(4):
                    turn(PS[:, 2 * (f % 2), 128 * n:128 * n + 128], rows_in[:, n, 128 * f:128 * f + 128], 128)
                turn(PS[:, 2 * (f % 2) + 1, 0:TS], rows_in[0:TS, 4, 128 * f:128 * f + 128], TS).then_inc(start_T.sem, 1)
            for f in range(KD):
                turn(PS[:, 4, NC * f:NC * f + NC], c_rows[:, 128 * f:128 * f + 128], NC)
            turn(PS[:, 4, 128:128 + KD], gf_rows[:], KD).then_inc(start_T.sem, 1)
            pe.wait_ge(start_ev.sem, KD)
            pe.wait_ge(cond_ready.sem, 1)

            def use(l, u):
                pe.wait_ge(lo_ready.sem, lo_ready.at(l, u + 1))

            def weights(part, slot, k, m):
                return part[:, slot, m * k:m * k + m]

            def products(slot, nk, xh, xl, k0, j, first=True, last=True, m=128):
                for k in range(nk):
                    for part, operands in ((whi, (xh, xl)), (wlo, (xh,))):
                        w = weights(part, slot, k, m)
                        for o in operands:
                            for half in range(2):
                                r = mm(PS[0:m, 2 * (j % 2) + half, 0:HT], w, o[:, k0 + k, half * HT:half * HT + HT],
                                       start=(first and k == 0 and part is whi and o is xh), stop=(last and k == nk - 1 and part is wlo))
                return r

            def dense(l, phase, u0, n, nk, xh, xl, base=0, first=0):
                with pe.Fori(first // 2, n // 2) as i:
                    for s in range(2):
                        use(l, 2 * i + (u0 + s))
                        pe.wait_ge(free[phase].sem, free[phase].at(l, 2 * i + (base + s - 1)))
                        products(s, nk, xh, xl, 0, s).then_inc(unit_used.sem, 1)

            def first_two(l, u0, tiles_before):
                use(l, u0 + 1)
                for k in range(KD):
                    pe.wait_ge(h_tile.sem, h_tile.at(l, tiles_before + k + 1))
                    for s in range(2):
                        for part, operands in ((whi, (h_hi, h_lo)), (wlo, (h_hi,))):
                            for o in operands:
                                for half in range(2):
                                    r = mm(PS[:, 2 * s + half, 0:HT], part[:, s, 128 * k:128 * k + 128], o[:, k, half * HT:half * HT + HT],
                                           start=k == 0 and part is whi and o is h_hi, stop=k == KD - 1 and part is wlo)
                        if k == KD - 1:
                            r.then_inc(unit_used.sem, 1)

            def banks_free_of(l, phase):
                pe.wait_ge(free[phase].sem, free[phase].at(l, N_TILE[phase]))
                pe.sem_inc(passed[3], 1)

            def over_partitions(l, src, k):
                pe.wait_ge(ssum.sem, ssum.at(l, k + 1))
                for half in range(2):
                    r = mm(PS[:, (0 if k == 0 else 6) + half, 0:HT], ones[:], src[:, half * HT:half * HT + HT], start=True, stop=True)
                r.then_inc(ssum_p.sem, 1)

            with pe.Fori(0, DEPTH) as l:
                def ada_pair(i, g):
                    for e in range(2):
                        s = 2 * g + e
                        pe.wait_ge(ada_in[s].sem, ada_in[s].at(l, 16 * (i + 1)))
                        if e == 0:
                            pe.wait_ge(ada_ev.sem, ada_ev.at(l, 3 * i + (g - 2)))
                        for k in range(KD):
                            r = mm(PS[0:NC, (4, 5, 7)[g], 128 * e:128 * e + 128], cond[:, k, :], ada_w[:, s, 128 * k:128 * k + 128],
                                   start=k == 0, stop=k == KD - 1)
                        r.then_inc(ada_used.sem, 1)
                    nc.tensor.drain().then_inc(ada_p.sem, 1)

                def ada_turn(i, g):
                    pe.wait_ge(ada_ev.sem, ada_ev.at(l, 3 * i + (g + 1)))
                    for e in range(2):
                        r = mm(PS[:, 6, bass.ds(NC * (6 * i + 2 * g + e), NC)], ada_rows[:, g, 128 * e:128 * e + 128], ident[0:NC, 0:NC],
                               start=True, stop=True)
                    r.then_inc(ada_T.sem, 1)

                pe.wait_ge(cl_ev.sem, cl_ev.at(l, 0))
                ada_pair(0, 0)
                ada_pair(0, 1)
                ada_pair(0, 2)
                pe.wait_ge(x_new.sem, x_new.at(l, 0))
                over_partitions(l, sumsq, 0)
                ada_turn(0, 0)
                ada_turn(0, 1)
                with pe.Fori(1, ADA // 6) as i:
                    ada_pair(i, 0)
                    ada_turn(i - 1, 2)
                    ada_pair(i, 1)
                    ada_turn(i, 0)
                    ada_pair(i, 2)
                    ada_turn(i, 1)
                ada_turn(ADA // 6 - 1, 2)

                pe.wait_ge(par_in.sem, par_in.at(l, 16 * PAR_LOADS))
                pe.wait_ge(root.sem, root.at(l, 1))
                turn(PS[:, 0, 0:80], rows[0:80, 0, :], 80)
                turn(PS[:, 0, 80:168], rows[0:88, 1, :], 88)
                turn(PS[:, 0, 168:256], rows[0:88, 2, :], 88)
                for c in range(4):
                    turn(PS[:, 1, 128 * c:128 * c + 128], rows[:, 3 + c, :], 128)
                turn(PS[:, 0, 256:384], rows[:, 7, :], 128)
                turn(PS[:, 0, 384:448], rows[0:64, 8, :], 64)
                for c in range(7):
                    turn(PS[:, 2 + c // 4, 128 * (c % 4):128 * (c % 4) + 128], rows[:, 9 + c, :], 128)
                turn(PS[:, 3, 384:448], rows[0:64, 16, :], 64).then_inc(par_T.sem, 1)
                pe.wait_ge(par_ev.sem, par_ev.at(l, 1))

                first_two(l, U_CQ, 0)
                dense(l, "qkv", U_CQ, 8, KD, h_hi, h_lo, first=2)
                pe.wait_ge(free["qkv"].sem, free["qkv"].at(l, 7))
                for s in range(2):
                    use(l, U_KR + s)
                    products(s, 4, h_hi, h_lo, 4 * s, 0, first=s == 0, last=s == 1, m=DR).then_inc(unit_used.sem, 1)
                banks_free_of(l, "qkv")
                dense(l, "u", U_U, 4, KD, h_hi, h_lo)
                over_partitions(l, sumsq, 1)
                pe.wait_ge(root.sem, root.at(l, 2))
                over_partitions(l, kv_sum[:, 0, :], 2)
                dense(l, "u", U_U + 4, 4, KD, h_hi, h_lo, 4)

                pe.wait_ge(root.sem, root.at(l, 3))
                pe.wait_ge(ckvn.sem, ckvn.at(l, 1))
                for n in range(5):
                    m = 128 if n < 4 else TS
                    if n >= 2:
                        pe.wait_ge(lat_ev.sem, lat_ev.at(l, n - 1))
                        pe.sem_inc(passed[3], 1)
                    for c in range(KC):
                        turn(PS[0:m, 4 + n % 2, 128 * c:128 * c + 128], ckv[:, c, 128 * n:128 * n + m], 128)
                    turn(PS[0:m, 4 + n % 2, KVL:LAT], krope[:, 128 * n:128 * n + m], DR).then_inc(lat_T.sem, 1)
                pe.wait_ge(lat_ev.sem, lat_ev.at(l, 5))
                pe.wait_ge(last_ready.sem, last_ready.at(l, 1))
                for f in range(KD):
                    o = 128 * (f % 4)
                    turn(PS[0:NB * CTX, 4 + f // 4, o:o + 128], pool_last[:, f, CTX:], 128)
                    r = turn(PS[0:CTX, 6 + f // 4, o:o + 128], pool_last[:, f, 0:CTX], 128)
                r.then_inc(last_T.sem, 1)

                pe.wait_ge(cqn.sem, cqn.at(l, 1))
                banks_free_of(l, "u")
                dense(l, "uq", U_QN, 8, KQ, cq_hi, cq_lo)
                dense(l, "uq", U_QR, 4, KQ, cq_hi, cq_lo, 8)

                def few_pieces(s, w0, step, xh, xl, out):
                    for k in range(2):
                        for part, operands in ((whi, (xh, xl)), (wlo, (xh,))):
                            for o in operands:
                                for bank, (c0, c1) in out:
                                    r = mm(PS[:, bank, 0:c1 - c0], part[:, s, w0 + step * k:w0 + step * k + 128], o[:, k, c0:c1],
                                           start=(k == 0 and part is whi and o is xh), stop=(k == 1 and part is wlo))
                    return r

                banks_free_of(l, "uq")
                pe.wait_ge(last_ev.sem, last_ev.at(l, 1))
                for g in range(4):
                    u = U_POOL + 3 * g
                    use(l, u)
                    pe.wait_ge(y_ready.sem, y_ready.at(l, g + 1))
                    for m in (2 * g, 2 * g + 1):
                        pe.wait_ge(free["pool"].sem, free["pool"].at(l, m - 1))
                        b = 4 + 2 * (m % 2)
                        few_pieces(u % 2, 128 * (m % 2), 256, y_hi[g], y_lo[g],
                                   ((b, (0, HT)), (b + 1, (HT, T)))).then_inc(full["pool"].sem, 1)
                    nc.tensor.drain().then_inc(unit_used.sem, 1)
                    for e in range(2):
                        use(l, u + 1 + e)
                        pe.wait_ge(free["g"].sem, free["g"].at(l, 2 * g + e - 1))
                        products((u + 1 + e) % 2, KD, h_hi, h_lo, 0, e).then_inc(unit_used.sem, 1)

                dense(l, "g", U_GB, 8, KD, h_hi, h_lo, 8)
                banks_free_of(l, "pool")

                banks_free_of(l, "g")
                for p in range(8):
                    s = p // 4
                    if p % 4 == 0:
                        use(l, U_UK + s)
                    pe.wait_ge(free["uk"].sem, free["uk"].at(l, p - 1))
                    b = 2 * (p % 2)
                    few_pieces(s, 128 * (p % 4), 512, ckv_hi, ckv_lo, ((b, (0, TP)),))
                    for k in range(2):
                        for part in (whi, wlo):
                            o = 512 * k + 128 * (p % 4)
                            r = mm(PS[:, b + 1, 128 * k:128 * k + 128], part[:, s, o:o + 128], ident_r[:], start=part is whi, stop=part is wlo)
                    r.then_inc(full["uk"].sem, 1)
                    if p % 4 == 3:
                        nc.tensor.drain().then_inc(unit_used.sem, 1)
                banks_free_of(l, "uk")
                for n in range(4):
                    s = n // 2
                    if n % 2 == 0:
                        use(l, U_UV + s)
                    pe.wait_ge(free["uv"].sem, free["uv"].at(l, n - 1))
                    for kb in (2 * (n % 2), 2 * (n % 2) + 1):
                        for k in range(2):
                            for o, parts in ((ckv_hi, (whi, wlo)), (ckv_lo, (whi,))):
                                for part in parts:
                                    r = mm(PS[:, kb, :], o[:, k, 128 * kb:128 * kb + 128], part[:, s, 512 * k:512 * k + 512],
                                           start=(k == 0 and o is ckv_hi and part is whi), stop=(k == 1 and o is ckv_lo))
                    r.then_inc(full["uv"].sem, 1)
                    if n % 2 == 1:
                        nc.tensor.drain().then_inc(unit_used.sem, 1)
                pe.wait_ge(lat_ev.sem, lat_ev.at(l, 5))
                for h in range(NH):
                    p, s = h // 2, 64 * (h % 2)
                    for c in range(KC):
                        r = mm(PS[:, 4 + 2 * c + h % 2, 64 * p:64 * p + 64], wukT[s:s + 64, p, 128 * c:128 * c + 128],
                               qn[s:s + 64, p, TP:T], start=True, stop=True)
                r.then_inc(qlat_p.sem, 1)

                def head_scores(h, s, blocks, first=False):
                    if blocks[0] == 0:
                        pe.wait_ge(q_asm.sem, q_asm.at(l, h + 1))
                        pe.wait_ge(k_asm.sem, k_asm.at(l, h + 1))
                    for qb in blocks:
                        if not first:
                            pe.wait_ge(expd.sem, expd.at(l, 4 * h + (qb - 3)))
                        mm(PS[:, qb, 0:128 * (qb + 1)], q96[:, s, 128 * qb:128 * qb + 128], k96[:, s, 0:128 * (qb + 1)],
                           start=True, stop=False)
                        mm(PS[:, qb, 128 * qb:128 * qb + 128], ident[:], causal[:], start=False, stop=True).then_inc(qk.sem, 1)

                def turn_probs(h):
                    pe.wait_ge(normed.sem, normed.at(l, h + 1))
                    pe.wait_ge(pt_ev.sem, pt_ev.at(l, h))
                    for kb in range(4):
                        for qb in range(kb, 4):
                            o = 64 * qb * (qb + 1) + 128 * kb
                            c = 128 * (qb - kb) + (256 if kb == 3 else 0)
                            r = turn(PS[:, 4 + min(kb, 2), c:c + 128], prob[:, o:o + 128], 128)
                    r.then_inc(pt_p.sem, 1)

                def head_values(h, s):
                    pe.wait_ge(pt_ev.sem, pt_ev.at(l, h + 1))
                    pe.wait_ge(v_asm.sem, v_asm.at(l, h + 1))
                    pe.wait_ge(o_done.sem, o_done.at(l, h))
                    for kb, o in enumerate((0, 512, 896, 1152)):
                        r = mm(PS[64 * s:64 * s + 64, 7, 128 * kb:TP], v64[:, s, kb, :], probT[:, o:o + TP - 128 * kb],
                               start=kb == 0, stop=kb == 3)
                    r.then_inc(pv.sem, 1)

                def head(h, s, last=False):
                    if not last:
                        head_scores(h + 1, 1 - s, (0, 1))
                    turn_probs(h)
                    if not last:
                        head_scores(h + 1, 1 - s, (2, 3))
                    head_values(h, s)

                pe.wait_ge(v_asm.sem, v_asm.at(l, 1))
                banks_free_of(l, "uv")
                pe.wait_ge(qlat_ev.sem, qlat_ev.at(l, 1))
                head_scores(0, 0, (0, 1, 2, 3), first=True)
                with pe.Fori(0, NH // 2 - 1) as i:
                    head(2 * i, 0)
                    head(2 * i + 1, 1)
                head(NH - 2, 0)
                head(NH - 1, 1, last=True)
                pe.wait_ge(o_done.sem, o_done.at(l, NH))
                pe.sem_inc(passed[3], 1)

                def turn_keys(b, s, g):
                    pe.wait_ge(kt_d.sem, kt_d.at(l, 4 * b + g))
                    pe.wait_ge(kt_a.sem, kt_a.at(l, 4 * b + g))
                    for j in range(4):
                        for c in range(KC):
                            turn(PS[:, c, 128 * j:128 * j + 128], pages[s][:, 4 * g + j, 128 * c:128 * c + 128], 128)
                        r = turn(PS[0:DR, 2, 128 * j:128 * j + 128], pages[s][:, 4 * g + j, KVL:LAT], 128)
                    r.then_inc(kt_p.sem, 1)

                def scores(b, s, g):
                    if g < 4:
                        pe.wait_ge(kt_d.sem, kt_d.at(l, 4 * b + (g + 1)))
                        pe.wait_ge(kt_a.sem, kt_a.at(l, 4 * b + (g + 1)))
                    pe.wait_ge(s_a.sem, s_a.at(l, 5 * b + (g - 1 if g >= 2 else 0)))
                    for c in range(3):
                        k = 128 if c < 2 else DR
                        if g < 4:
                            keys, w = keysT[g % 2][0:k, c, :], 512
                        else:
                            keys, w = (ckv[:, c, bass.ds(TP + NS * b, NS)] if c < 2 else krope[:, bass.ds(TP + NS * b, NS)]), NS
                        r = mm(PS[:, 3 + g % 2, 0:w], qst[0:k, s, c, :], keys, start=c == 0, stop=c == 2)
                    r.then_inc(s_p.sem, 1)

                def turn_output(b):
                    pe.wait_ge(so_d.sem, so_d.at(l, b + 1))
                    for c in range(KC):
                        r = turn(PS[:, 7, 256 + 128 * c:384 + 128 * c], olat[:, 128 * c:128 * c + 128], 128)
                    r.then_inc(so_T.sem, 1)

                def sequence(i, s, first=False, last=False):
                    b = 2 * i + s
                    pe.wait_ge(qst_ready.sem, qst_ready.at(l, b + 1))
                    for g in range(4):
                        if g < 3:
                            pe.wait_ge(pages_in[s][g + 1].sem, pages_in[s][g + 1].at(l, 16 * 4 * (i + 1)))
                            turn_keys(b, s, g + 1)
                        scores(b, s, g)
                        if g == 0 and not first:
                            turn_output(b - 1)
                    scores(b, s, 4)
                    if not last:
                        pe.wait_ge(pages_in[1 - s][0].sem, pages_in[1 - s][0].at(l, 16 * 4 * (i + (1 + s))))
                        turn_keys(b + 1, 1 - s, 0)
                    pe.wait_ge(s_exp.sem, s_exp.at(l, b + 1))
                    for g in range(5):
                        e, k = ((spt_d, 3 * b), (spt_d, 3 * b), (spt_a, 2 * b + 1), (spt_d, 3 * b + 1), (spt_a, 2 * b + 2))[g]
                        pe.wait_ge(e.sem, e.at(l, k))
                        if g < 4:
                            for j in range(4):
                                o = 512 * g + 128 * j
                                r = turn(PS[:, 5 + g % 2, 128 * j:128 * j + 128], sc[:, o:o + 128], 128)
                        else:
                            r = turn(PS[0:NS, 5, 0:128], sc[:, PAST:PAST + NS], 128)
                        r.then_inc(spt_p.sem, 1)
                    pe.wait_ge(spt_a.sem, spt_a.at(l, 2 * b + 2))
                    pe.wait_ge(spt_d.sem, spt_d.at(l, 3 * b + 3))
                    pe.wait_ge(new_in[s].sem, new_in[s].at(l, 16 * (i + 1)))
                    pe.wait_ge(so_a.sem, so_a.at(l, b))
                    for j in range(NPG):
                        mm(PS[:, 7, 0:KVL], pT[:, j, :], pages[s][:, j, 0:KVL], start=j == 0, stop=False)
                    mm(PS[:, 7, 0:KVL], pT[0:NS, NPG, :], newk[:, s, 0:KVL], start=False, stop=True).then_inc(spv.sem, 1)

                pe.wait_ge(pages_in[0][0].sem, pages_in[0][0].at(l, 16 * 4))
                turn_keys(0, 0, 0)
                sequence(0, 0, first=True)
                sequence(0, 1)
                with pe.Fori(1, NB // 2 - 1) as i:
                    sequence(i, 0)
                    sequence(i, 1)
                sequence(NB // 2 - 1, 0)
                sequence(NB // 2 - 1, 1, last=True)
                turn_output(NB - 1)
                pe.wait_ge(so_a.sem, so_a.at(l, NB))
                pe.wait_ge(wuv_in.sem, wuv_in.at(l, 16))
                for h in range(NH):
                    p, s = h // 2, 64 * (h % 2)
                    for c in range(KC):
                        r = mm(PS[s:s + 64, 0, 64 * p:64 * p + 64], wuv[:, c, DV * h:DV * h + DV], olatT[:, c, h].rearrange("p b s -> p (b s)"),
                               start=c == 0, stop=c == KC - 1)
                r.then_inc(uvs.sem, 1)

                first_two(l, U_OUT, KD)
                dense(l, "out", U_OUT, 8, KD, h_hi, h_lo, first=2)
                over_partitions(l, sumsq, 3)
                banks_free_of(l, "out")
                first_two(l, U_UP, 2 * KD)
                dense(l, "up", U_UP, 44, KD, h_hi, h_lo, first=2)
                pe.wait_ge(silud.sem, silud.at(l, KF))
                for n in range(11):
                    if n >= 4:
                        pe.wait_ge(cl_ev.sem, cl_ev.at(l, n - 3))
                    for f in range(4 * n, 4 * n + 4):
                        r = turn(PS[0:2 * NC, 4 + n % 4, 128 * (f % 4):128 * (f % 4) + 128], conv_last[:, f, :], 128)
                    r.then_inc(cl_T.sem, 1)
                pe.wait_ge(act_ready.sem, act_ready.at(l, KF))
                banks_free_of(l, "up")
                with pe.Fori(0, 4) as i:
                    for t in range(2):
                        pe.wait_ge(free["down"].sem, free["down"].at(l, 2 * i + (t - 1)))
                        for c in range(3):
                            w = 3 * t + c
                            use(l, 6 * i + (U_DOWN + w))
                            products(w % 2, min(8, KF - 8 * c), act_hi, act_lo, 8 * c, t, first=c == 0, last=c == 2).then_inc(unit_used.sem, 1)

            pe.wait_ge(x_new.sem, x_new.at(DEPTH, 0))
            over_partitions(DEPTH, sumsq, 0)
            pe.wait_ge(fin_norm.sem, 1)
            for n in range(5):
                m = 128 if n < 4 else TS
                if n >= 2:
                    pe.wait_ge(fin_ev.sem, n - 1)
                for f in range(KD):
                    o = 128 * (f % 4)
                    r = turn(PS[0:m, 2 * (n % 2) + f // 4, o:o + 128], yT[:, f, 128 * n:128 * n + m], 128)
                r.then_inc(fin_T.sem, 1)


_ORDER = ["x_prompt", "x_sample", "cache_latent", "state_pool", "state_conv", "page_table", "c_prompt", "c_sample",
          "w_ada", "b_ada", "g_attn", "w_in", "g_q", "w_uq", "g_kv", "w_uk", "w_uv", "w_pool", "pool_scale", "w_out",
          "g_ffn", "w_up", "w_conv", "b_conv", "w_down", "g_final"]
_OUT = [("y_p", (1, TP, D)), ("y_s", (NB, NS, D)), ("lat_p", (DEPTH, 1, TP, LAT)), ("pool_p", (DEPTH, 1, CTX, D)),
        ("conv_p", (DEPTH, 1, 2, 2 * DF)), ("lat_s", (DEPTH, NB, NS, LAT)), ("pool_s", (DEPTH, NB, CTX, D)),
        ("conv_s", (DEPTH, NB, 2, 2 * DF))]


def constants():
    tok = np.arange(128)
    half = DR // 2
    freq = np.float32(10000.0) ** (-np.arange(half, dtype=np.float32) / np.float32(half))
    pos = np.concatenate([np.arange(TP), np.tile(PAST + np.arange(NS), NB)]).astype(np.float32)
    ang = (pos[None, :] * freq[:, None]).astype(np.float32)
    cos, sin = np.cos(ang), np.sin(ang)
    rope = np.stack([np.tile(np.concatenate([cos, cos]), (4, 1)), np.tile(np.concatenate([-sin, sin]), (4, 1))], 1)
    ramp = np.ones((4, 16), np.float32)
    for g, w in enumerate(WINDOWS):
        ramp[g, :15] = w / np.minimum(np.arange(15) + 1.0, w)
    return {
        "ident": np.eye(128, dtype=np.float32),
        "ones": np.ones((128, 128), np.float32),
        "causal": np.where(tok[None, :] <= tok[:, None], 0, -1e30).astype(np.float32),
        "causal_s": np.where(np.arange(NS)[None, :] <= (tok % NS)[:, None], 0, -1e30).astype(np.float32),
        "ramp": np.tile(ramp.reshape(1, 64), (128, 1)).astype(np.float32),
        "rope": np.ascontiguousarray(rope.reshape(128, 2 * T)).astype(np.float32),
    }


def kernel(**inputs):
    import concourse.bacc as bacc
    from concourse.bass_utils import run_bass_kernel_spmd

    nc = bacc.Bacc("TRN2", target_bir_lowering=False, num_devices=1)
    arrays, A, O = {}, {}, {}
    for name in _ORDER:
        arrays[name] = np.ascontiguousarray(inputs[name])
    for name, a in constants().items():
        arrays["t_" + name] = a
    for name, a in arrays.items():
        A[name.removeprefix("t_")] = nc.dram_tensor(name, a.shape, mybir.dt.from_np(a.dtype), kind="ExternalInput").ap()
    for name, shape in _OUT:
        O[name] = nc.dram_tensor("o_" + name, shape, F32, kind="ExternalOutput").ap()
    build(nc, A, O)
    r = run_bass_kernel_spmd(nc, [arrays], core_ids=[0]).results[0]
    return tuple(r["o_" + name] for name, _ in _OUT)
```
